# Optimizing a Trainium2 kernel written in Bass

```python
import math
import jax, jax.numpy as jnp
from jax import lax
import numpy as np

D_MODEL = 1024
BATCH = 1
SEQ = 512
DEPTH = 2

N_MIXERS = 2
N_SSM_LAYERS = (DEPTH + 1) // 2
N_ATTN_LAYERS = DEPTH // 2
SSM_EXPAND = 2
D_INNER = SSM_EXPAND * D_MODEL
SSM_HEAD_DIM = 64
SSM_HEADS = D_INNER // SSM_HEAD_DIM
SSM_GROUPS = 8
SSM_STATE = 128
SSM_CONV = 4
SSM_CHUNK = 128
SSM_CONV_DIM = D_INNER + 2 * SSM_GROUPS * SSM_STATE
SSM_IN_DIM = 2 * D_INNER + 2 * SSM_GROUPS * SSM_STATE + SSM_HEADS
ATTN_HEAD_DIM = 64
ATTN_HEADS = D_MODEL // (2 * ATTN_HEAD_DIM)
ATTN_V_DIM = 2 * ATTN_HEAD_DIM
Q_BLOCK = 128
D_FF = 2816
FFN_CONV = 3
RMS_EPS = 1e-6

kernel_name = "hybrid_ssd_diffattn_convffn"

def rmsnorm(x, g):
    xf = x.astype(jnp.float32)
    y = xf * lax.rsqrt(jnp.mean(xf * xf, axis=-1, keepdims=True) + RMS_EPS)
    return (y * g.astype(jnp.float32)).astype(x.dtype)

def causal_dwconv(x, w, b):
    k_w = w.shape[0]
    s = x.shape[1]
    xp = jnp.pad(x, ((0, 0), (k_w - 1, 0), (0, 0)))
    y = xp[:, 0:s] * w[0]
    for k in range(1, k_w):
        y = y + xp[:, k:k + s] * w[k]
    return y + b

def ssd_chunked(xh, dA, Bm, Cm):
    b, s, h, p = xh.shape
    g, n = Bm.shape[2], Bm.shape[3]
    r = h // g
    l = SSM_CHUNK
    c = s // l
    x = xh.reshape(b, c, l, g, r, p)
    A = dA.reshape(b, c, l, g, r).transpose(0, 1, 3, 4, 2)
    Bc = Bm.reshape(b, c, l, g, n)
    Cc = Cm.reshape(b, c, l, g, n)
    A_cs = jnp.cumsum(A, axis=-1)
    causal = jnp.tril(jnp.ones((l, l), dtype=bool))
    seg = A_cs[..., :, None] - A_cs[..., None, :]
    L = jnp.exp(jnp.where(causal, seg, -jnp.inf))
    CB = jnp.einsum('bclgn,bcsgn->bcgls', Cc, Bc)
    y_diag = jnp.einsum('bcgls,bcgrls,bcsgrp->bclgrp', CB, L, x)
    decay = jnp.exp(A_cs[..., -1:] - A_cs)
    states = jnp.einsum('bcsgn,bcgrs,bcsgrp->bcgrpn', Bc, decay, x)
    chunk_decay = jnp.exp(A_cs[..., -1])

    def step(carry, inp):
        st, dec = inp
        return carry * dec[..., None, None] + st, carry

    init = jnp.zeros_like(states[:, 0])
    _, prev = lax.scan(step, init, (states.transpose(1, 0, 2, 3, 4, 5),
                                    chunk_decay.transpose(1, 0, 2, 3)))
    prev = prev.transpose(1, 0, 2, 3, 4, 5)
    y_off = jnp.einsum('bclgn,bcgrpn,bcgrl->bclgrp', Cc, prev, jnp.exp(A_cs))
    return (y_diag + y_off).reshape(b, s, h, p)

def mamba2_mixer(u, w_in, conv_w, conv_b, dt_bias, A_log, D_skip, norm_g, w_out):
    b, s, _ = u.shape
    f32 = jnp.float32
    proj = jnp.einsum('bsd,de->bse', u, w_in)
    z, xBC, dt = jnp.split(proj, [D_INNER, D_INNER + SSM_CONV_DIM], axis=-1)
    xBC = jax.nn.silu(causal_dwconv(xBC, conv_w, conv_b))
    xs, Bm, Cm = jnp.split(xBC, [D_INNER, D_INNER + SSM_GROUPS * SSM_STATE], axis=-1)
    xs = xs.reshape(b, s, SSM_HEADS, SSM_HEAD_DIM).astype(f32)
    Bm = Bm.reshape(b, s, SSM_GROUPS, SSM_STATE).astype(f32)
    Cm = Cm.reshape(b, s, SSM_GROUPS, SSM_STATE).astype(f32)
    dt = jax.nn.softplus(dt.astype(f32) + dt_bias.astype(f32))
    A = -jnp.exp(A_log.astype(f32))
    y = ssd_chunked(xs * dt[..., None], dt * A, Bm, Cm)
    y = y + xs * D_skip.astype(f32)[:, None]
    y = y.reshape(b, s, D_INNER) * jax.nn.silu(z.astype(f32))
    yg = y.reshape(b, s, SSM_GROUPS, D_INNER // SSM_GROUPS)
    yg = yg * lax.rsqrt(jnp.mean(yg * yg, axis=-1, keepdims=True) + RMS_EPS)
    y = yg.reshape(b, s, D_INNER) * norm_g.astype(f32)
    return jnp.einsum('bse,ed->bsd', y.astype(u.dtype), w_out)

def alibi_slopes(h):
    return jnp.exp2(-8.0 * jnp.arange(1, h + 1, dtype=jnp.float32) / h)

def diff_attention(u, w_qkv, lq1, lk1, lq2, lk2, subln_g, w_out, lambda_init):
    b, s, _ = u.shape
    f32 = jnp.float32
    H, dh = ATTN_HEADS, ATTN_HEAD_DIM
    qkv = jnp.einsum('bsd,de->bse', u, w_qkv)
    q, k, v = jnp.split(qkv, 3, axis=-1)
    q = q.reshape(b, s, H, 2, dh)
    k = k.reshape(b, s, H, 2, dh)
    v = v.reshape(b, s, H, ATTN_V_DIM)
    lam = (jnp.exp(jnp.sum(lq1.astype(f32) * lk1.astype(f32)))
           - jnp.exp(jnp.sum(lq2.astype(f32) * lk2.astype(f32))) + lambda_init)
    scale = dh ** -0.5
    slopes = alibi_slopes(H)
    kpos = jnp.arange(s)
    n_blk = s // Q_BLOCK

    def block(i):
        start = i * Q_BLOCK
        qb = lax.dynamic_slice_in_dim(q, start, Q_BLOCK, axis=1)
        sc = jnp.einsum('bqhtd,bkhtd->bhtqk', qb, k).astype(f32) * scale
        qpos = start + jnp.arange(Q_BLOCK)
        dist = (qpos[:, None] - kpos[None, :]).astype(f32)
        bias = -slopes[:, None, None, None] * dist
        sc = jnp.where(dist >= 0, sc + bias, -jnp.inf)
        pr = jax.nn.softmax(sc, axis=-1)
        a = pr[:, :, 0] - lam * pr[:, :, 1]
        return jnp.einsum('bhqk,bkhe->bqhe', a.astype(v.dtype), v)

    out = lax.map(block, jnp.arange(n_blk))
    out = out.transpose(1, 0, 2, 3, 4).reshape(b, s, H, ATTN_V_DIM)
    out = rmsnorm(out, subln_g) * (1.0 - lambda_init)
    return jnp.einsum('bse,ed->bsd', out.reshape(b, s, H * ATTN_V_DIM), w_out)

def conv_ffn(u, w_up, conv_w, conv_b, w_down):
    h = jnp.einsum('bsd,df->bsf', u, w_up)
    h = causal_dwconv(h, conv_w, conv_b)
    gate, up = jnp.split(h, 2, axis=-1)
    return jnp.einsum('bsf,fd->bsd', jax.nn.silu(gate) * up, w_down)

def setup_inputs(seed: int = 0) -> dict:
    key = jax.random.key(seed)
    ks = jax.random.split(key, 24)
    f32 = jnp.float32

    def nrm(k, shape, scale):
        return jax.random.normal(k, shape, f32) * scale

    NS, NA = N_SSM_LAYERS, N_ATTN_LAYERS
    dt0 = jnp.exp(jax.random.uniform(ks[4], (NS, SSM_HEADS), f32, math.log(1e-3), math.log(1e-1)))
    return {
        "x": nrm(ks[0], (BATCH, SEQ, D_MODEL), 1.0),
        "ssm_w_in": nrm(ks[1], (NS, D_MODEL, SSM_IN_DIM), D_MODEL ** -0.5),
        "ssm_conv_w": nrm(ks[2], (NS, SSM_CONV, SSM_CONV_DIM), SSM_CONV ** -0.5),
        "ssm_conv_b": nrm(ks[3], (NS, SSM_CONV_DIM), 0.02),
        "ssm_dt_bias": dt0 + jnp.log(-jnp.expm1(-dt0)),
        "ssm_A_log": jnp.log(jax.random.uniform(ks[5], (NS, SSM_HEADS), f32, 1.0, 16.0)),
        "ssm_D": 1.0 + nrm(ks[6], (NS, SSM_HEADS), 0.1),
        "ssm_norm_g": 1.0 + nrm(ks[7], (NS, D_INNER), 0.1),
        "ssm_w_out": nrm(ks[8], (NS, D_INNER, D_MODEL), D_INNER ** -0.5),
        "attn_w_qkv": nrm(ks[9], (NA, D_MODEL, 3 * D_MODEL), D_MODEL ** -0.5),
        "attn_lambda_q1": nrm(ks[10], (NA, ATTN_HEAD_DIM), 0.1),
        "attn_lambda_k1": nrm(ks[11], (NA, ATTN_HEAD_DIM), 0.1),
        "attn_lambda_q2": nrm(ks[12], (NA, ATTN_HEAD_DIM), 0.1),
        "attn_lambda_k2": nrm(ks[13], (NA, ATTN_HEAD_DIM), 0.1),
        "attn_subln_g": 1.0 + nrm(ks[14], (NA, ATTN_V_DIM), 0.1),
        "attn_w_out": nrm(ks[15], (NA, D_MODEL, D_MODEL), D_MODEL ** -0.5),
        "norm_mix_pre": 1.0 + nrm(ks[16], (DEPTH, D_MODEL), 0.1),
        "norm_mix_post": 1.0 + nrm(ks[17], (DEPTH, D_MODEL), 0.1),
        "norm_ffn_pre": 1.0 + nrm(ks[18], (DEPTH, D_MODEL), 0.1),
        "norm_ffn_post": 1.0 + nrm(ks[19], (DEPTH, D_MODEL), 0.1),
        "ffn_w_up": nrm(ks[20], (DEPTH, D_MODEL, 2 * D_FF), D_MODEL ** -0.5),
        "ffn_conv_w": nrm(ks[21], (DEPTH, FFN_CONV, 2 * D_FF), FFN_CONV ** -0.5),
        "ffn_conv_b": nrm(ks[22], (DEPTH, 2 * D_FF), 0.02),
        "ffn_w_down": nrm(ks[23], (DEPTH, D_FF, D_MODEL), D_FF ** -0.5),
    }

def reference(x, ssm_w_in, ssm_conv_w, ssm_conv_b, ssm_dt_bias, ssm_A_log, ssm_D, ssm_norm_g,
              ssm_w_out, attn_w_qkv, attn_lambda_q1, attn_lambda_k1, attn_lambda_q2,
              attn_lambda_k2, attn_subln_g, attn_w_out, norm_mix_pre, norm_mix_post,
              norm_ffn_pre, norm_ffn_post, ffn_w_up, ffn_conv_w, ffn_conv_b, ffn_w_down):
    for i in range(DEPTH):
        j = i // N_MIXERS
        hn = rmsnorm(x, norm_mix_pre[i])
        if i % N_MIXERS == 0:
            m = mamba2_mixer(hn, ssm_w_in[j], ssm_conv_w[j], ssm_conv_b[j], ssm_dt_bias[j],
                             ssm_A_log[j], ssm_D[j], ssm_norm_g[j], ssm_w_out[j])
        else:
            lambda_init = 0.8 - 0.6 * math.exp(-0.3 * i)
            m = diff_attention(hn, attn_w_qkv[j], attn_lambda_q1[j], attn_lambda_k1[j],
                               attn_lambda_q2[j], attn_lambda_k2[j], attn_subln_g[j],
                               attn_w_out[j], lambda_init)
        x = x + rmsnorm(m, norm_mix_post[i])
        hn = rmsnorm(x, norm_ffn_pre[i])
        f = conv_ffn(hn, ffn_w_up[i], ffn_conv_w[i], ffn_conv_b[i], ffn_w_down[i])
        x = x + rmsnorm(f, norm_ffn_post[i])
    return x


_drawn_inputs = setup_inputs


def setup_inputs(seed=0):
    import zlib

    import numpy as np

    out = dict(_drawn_inputs(seed))
    spreads = {}
    factors = {}
    for name, (base, spread) in spreads.items():
        noise = np.random.default_rng([zlib.crc32(name.encode()), seed]).standard_normal(out[name].shape)
        drawn = base * np.exp(spread * noise) if base else spread * noise
        out[name] = __import__('jax').numpy.asarray(drawn.astype(out[name].dtype))
    for name, factor in factors.items():
        out[name] = (out[name] * factor).astype(out[name].dtype)
    return out
```

```python
import math
from contextlib import ExitStack, contextmanager

import numpy as np

import concourse.bass as bass
from concourse import mybir

F32 = mybir.dt.float32
F32R = mybir.dt.float32r
ALU = mybir.AluOpType
ACT = mybir.ActivationFunctionType
AX = mybir.AxisListType

P = 128
S = 512
NB = S // P
D = 1024
KC = D // P
DI = 2 * D
YC = DI // P
NG, HG, HD = 8, 4, 64
HS = NG * HG
SSM_T, FFN_T = 4, 3
NH, DH = 8, 64
DFF = 2816
FC = DFF // P
HU = FC // 2
UW = HU * P
EPS = 1e-6
LAMBDA_INIT = 0.8 - 0.6 * math.exp(-0.3 * 1)
MASKED = -1e30

NORM0 = 0
SSM0 = NORM0 + 8 * KC
SSMW = 4 * (SSM_T + 1) + 4
FFN0 = SSM0 + NG * SSMW
FFNW = 2 * (FFN_T + 1)
SUBLN = FFN0 + 2 * FC * FFNW
DTB = SUBLN + 1
ALOG = DTB + 1
NPAR = ALOG + 1


class Phase:

    def __init__(self, units, chunks, width, kind, prev):
        self.units, self.chunks, self.width, self.kind, self.prev = units, chunks, width, kind, prev
        self.U0 = prev.U0 + prev.units if prev else 0
        self.Q0 = prev.Q0 + prev.chunks if prev else 0
        self.before = {"in": 0, "out": 0}
        if prev:
            self.before = dict(prev.before)
            self.before[prev.kind] += prev.chunks


def phases():
    made, prev = [], None
    for units, chunks, width, kind in (
            (1 + 6 * NG, 1 + 6 * NG, KC * P, "in"), (2 * KC, KC, KC * P, "out"),
            (2 * FC, 2 * FC, KC * P, "in"), (2 * KC, KC, UW, "out"),
            (3 * NH, 3 * NH, KC * P, "in"), (KC, KC, KC * P, "out"),
            (2 * FC, 2 * FC, KC * P, "in"), (2 * KC, KC, UW, "out")):
        prev = Phase(units, chunks, width, kind, prev)
        made.append(prev)
    return made


class Chain:

    def __init__(self, sem):
        self.sem, self.n, self.dyn = sem, 0, 0

    def __call__(self, ins):
        ins.then_inc(self.sem, 1)
        self.n += 1

    def value(self):
        return self.n + self.dyn

    @contextmanager
    def loop(self, i, start, trips, per):
        first = self.n
        self.dyn = (i - start) * per
        yield
        assert self.n - first == per, (self.n - first, per)
        self.dyn = 0
        self.n = first + per * trips


def trunk(nc, x_in, w_mix, w_sout, w_up0, w_dn0, w_qkv, w_aout, w_up1, w_dn1, params, lam_in, out):
    ctx = ExitStack()
    with ctx:
        MIX, SOUT, UP0, DN0, QKV, AOUT, UP1, DN1 = PH = phases()
        dram_of = dict(zip(PH, (w_mix, w_sout, w_up0, w_dn0, w_qkv, w_aout, w_up1, w_dn1)))

        def sb(name, shape, dt=F32, scope=ctx):
            return scope.enter_context(nc.sbuf_tensor(name, shape, dt))

        def sem(name):
            return ctx.enter_context(nc.semaphore(name))

        x = sb("x", [P, KC, S])
        raw = sb("raw", [P, 2, UW])
        w_hi = sb("w_hi", [P, 2, UW], F32R)
        w_lo = sb("w_lo", [P, 2, UW], F32R)
        par = sb("par", [P, NPAR])
        lam_v = sb("lam_v", [P, 4 * DH])
        lam_p = sb("lam_p", [P, 2 * DH])
        lam_s = sb("lam_s", [P, 8])
        gsub = sb("gsub", [P, 1])
        slopes = sb("slopes", [P, NH])
        eps = sb("eps", [P, 1])
        ident = sb("ident", [P, P])
        ones = sb("ones", [P, P])
        mean_col = sb("mean_col", [P, 3])
        root = sb("root", [P, NB])
        rcol = sb("rcol", [P, NB])
        diag = sb("diag", [P, NB, P])
        r_pre = sb("r_pre", [P, S])
        ssq = sb("ssq", [P, S])
        sq = sb("sq", [P, 2, S])
        hn_lo = sb("hn_lo", [P, KC, S], F32R)
        with ExitStack() as lap:
            mbuf = sb("mbuf", [P, KC, S], scope=lap)
        hn_hi = sb("hn_hi", [P, KC, S], F32R)

        with ExitStack() as ssm:
            with ExitStack() as lap:
                ybuf = sb("ybuf", [P, YC, S], scope=lap)
            y_lo = sb("y_lo", [P, YC, S], F32R, scope=ssm)
            with ExitStack() as lap:
                acs_bc = sb("acs_bc", [P, HG, S], scope=lap)
                ecs_bc = sb("ecs_bc", [P, HG, S], scope=lap)
                xc = sb("xc", [P, 2, S], scope=lap)
                bT = sb("bT", [P, S], scope=lap)
                cT = sb("cT", [P, S], scope=lap)
                ug_s = sb("ug_s", [P, SSM_T - 1 + S], scope=lap)
                cv_s = sb("cv_s", [P, S], scope=lap)
                btok = sb("btok", [P, NB, P], scope=lap)
                xdd = sb("xdd", [P, NB, HG, HD], scope=lap)
            y_hi = sb("y_hi", [P, YC, S], F32R, scope=ssm)
            sb("gap", [P, 1024], scope=ssm)
            with ExitStack() as lap:
                d_v = sb("d_v", [HS, S], scope=lap)
                d_e = sb("d_e", [HS, S], scope=lap)
                d_z = sb("d_z", [HS, S], scope=lap)
                d_w = sb("d_w", [HS, S], scope=lap)
                d_p = sb("d_p", [HS, S], scope=lap)
                d_dt = sb("d_dt", [HS, S], scope=lap)
                d_acs = sb("d_acs", [HS, S], scope=lap)
                d_ea = sb("d_ea", [HS, 1], scope=lap)
                last_row = sb("last_row", [P, P], scope=lap)
            xdt = sb("xdt", [P, NB, HG, HD], scope=ssm)
            m_t = sb("m_t", [P, HG, S], scope=ssm)
            cs_t = sb("cs_t", [P, HG, S - P], scope=ssm)
            cbm = sb("cbm", [P, S], scope=ssm)
            prev = sb("prev", [P, NB - 1, HG, HD], scope=ssm)
            pdec = sb("pdec", [P, HG, HD], scope=ssm)
            yt = sb("yt", [P, 2, S], scope=ssm)
            zs = sb("zs", [P, 2, S], scope=ssm)
            tri = sb("tri", [P, P], scope=ssm)
            dt_tok = sb("dt_tok", [P, NB, HS], scope=ssm)
            nacs = sb("nacs", [P, NB, HS], scope=ssm)
            acs_tok = sb("acs_tok", [P, NB, HS], scope=ssm)
            wdec = sb("wdec", [P, NB, HS], scope=ssm)
            nac_g = sb("nac_g", [P, NB, HG], scope=ssm)
        with ExitStack() as ffn:
            h_hi = sb("h_hi", [P, FC, S], F32R, scope=ffn)
            h_lo = sb("h_lo", [P, FC, S], F32R, scope=ffn)
            ug_f = sb("ug_f", [P, FFN_T - 1 + S], scope=ffn)
            cg = sb("cg", [P, S], scope=ffn)
            cu = sb("cu", [P, S], scope=ffn)
            sg = sb("sg", [P, S], scope=ffn)
            hb = sb("hb", [P, S], scope=ffn)
        with ExitStack() as att:
            o_hi = sb("o_hi", [P, NH, S], F32R, scope=att)
            o_lo = sb("o_lo", [P, NH, S], F32R, scope=att)
            qT = sb("qT", [P, 2, S], scope=att)
            kT = sb("kT", [P, 2, S], scope=att)
            vT = sb("vT", [P, 2, S], scope=att)
            vtok = sb("vtok", [P, 2, NB, P], scope=att)
            dist_i = sb("dist_i", [P, S], mybir.dt.int32, scope=att)
            dist = sb("dist", [P, S], scope=att)
            sc = sb("sc", [P, 2, 2, S], scope=att)
            pr = sb("pr", [P, 2, 2, S], scope=att)
            at = sb("at", [P, 2, S], scope=att)
            aT = sb("aT", [P, NB, S], scope=att)
            ob = sb("ob", [P, S], scope=att)
            osq = sb("osq", [P, S], scope=att)
            on = sb("on", [P, S], scope=att)
            nmx = sb("nmx", [P, 2, 2], scope=att)
            den = sb("den", [P, 2, 2], scope=att)
            cf = sb("cf", [P, 2, 2], scope=att)

        bank = [ctx.enter_context(nc.psum_tensor(f"bank{i}", [P, S], F32)) for i in range(2)]
        b_norm = ctx.enter_context(nc.psum_tensor("b_norm", [P, S], F32))
        b_x = ctx.enter_context(nc.psum_tensor("b_x", [P, 2, S], F32))
        b_cb = ctx.enter_context(nc.psum_tensor("b_cb", [P, S], F32))
        b_y = ctx.enter_context(nc.psum_tensor("b_y", [P, 2, S], F32))
        scores_in = (b_x, b_y)
        b_tr, b_pv = b_cb, b_norm

        scratch = nc.dram_tensor("scratch", [2, HS, S], F32).ap()

        par_in, lam_in_s, x_in_s = sem("par_in"), sem("lam_in_s"), sem("x_in_s")
        raw_in = [sem("raw_in0"), sem("raw_in1")]
        acs_out, ecs_out, acs_in, ecs_in = sem("acs_out"), sem("ecs_out"), sem("acs_in"), sem("ecs_in")
        y_sent = sem("y_sent")
        hi_made, lo_made, unit_done = sem("hi_made"), sem("lo_made"), sem("unit_done")
        evac = {"in": sem("evac_in"), "out": sem("evac_out")}
        dve_done = sem("dve_done")
        consts = sem("consts")
        sq_ready, sq_added = sem("sq_ready"), sem("sq_added")
        stat_ready, root_ready, diag_ready, bc_ready = (
            sem("stat_ready"), sem("root_ready"), sem("diag_ready"), sem("bc_ready"))
        rpre_copied = sem("rpre_copied")
        x_new, hnhi_ready, hnlo_ready = sem("x_new"), sem("hnhi_ready"), sem("hnlo_ready")
        conv_ready = sem("conv_ready")
        dt_in, dt_exp, al_exp, acs_ready, ecs_ready = (
            sem("dt_in"), sem("dt_exp"), sem("al_exp"), sem("acs_ready"), sem("ecs_ready"))
        dtr_ready, tok_ready, tot_ready, dec_in, dec_exp = (
            sem("dtr_ready"), sem("tok_ready"), sem("tot_ready"), sem("dec_in"), sem("dec_exp"))
        silu_ready = sem("silu_ready")
        trb_ready, trx_ready, cb_ready, st_ready, y_ready = (
            sem("trb_ready"), sem("trx_ready"), sem("cb_ready"), sem("st_ready"), sem("y_ready"))
        btok_ready, skip_ready, seg_ready, seg_exp = (
            sem("btok_ready"), sem("skip_ready"), sem("seg_ready"), sem("seg_exp"))
        xw_ready, cbm_ready, prev_ready, m_ready, cs_ready = (
            sem("xw_ready"), sem("cbm_ready"), sem("prev_ready"), sem("m_ready"), sem("cs_ready"))
        y_gated, ysq_ready, y_normed = sem("y_gated"), sem("ysq_ready"), sem("y_normed")
        yhi_ready, ylo_ready = sem("yhi_ready"), sem("ylo_ready")
        gate_ready, hb_ready, hhi_ready, hlo_ready = (
            sem("gate_ready"), sem("hb_ready"), sem("hhi_ready"), sem("hlo_ready"))
        s_ready, s_taken, mx_ready, p_ready, a_ready, tr_ready, tr_copied = (
            sem("s_ready"), sem("s_taken"), sem("mx_ready"), sem("p_ready"),
            sem("a_ready"), sem("tr_ready"), sem("tr_copied"))
        pv_ready, ob_ready, on_ready, ohi_ready, olo_ready = (
            sem("pv_ready"), sem("ob_ready"), sem("on_ready"), sem("ohi_ready"), sem("olo_ready"))
        lam_dots, lam_exps, dist_made = sem("lam_dots"), sem("lam_exps"), sem("dist_made")

        ch = Chain(dve_done)
        N_CONST = 19
        MIX_CHAIN = 4 * (SSM_T - 1) + 8
        ATT_CHAIN = 2 * (4 * 3 + 1)

        order = ["pre0", "group"] + ["post1", "pre1", "post2", "pre2", "head"] + ["post3", "pre3", "post4"]
        norm_no, n = {}, 0
        for name in order:
            norm_no[name] = n
            n += {"group": NG, "head": NH}.get(name, 1)
        sum_no = {name: n for n, name in enumerate(x for x in order if x not in ("group", "head"))}

        def gain(layer, kind, m):
            c = NORM0 + (layer * 4 + kind) * KC + m
            return par[:, c:c + 1]

        def col(c):
            return par[:, bass.ds(c, 1)]

        def slot_of(ph, j):
            return (ph.U0 + j) % 2

        def acc_of(ph, j):
            return bank[(ph.Q0 + j) % 2]

        def load_unit(sp, ph, j, rep):
            slot = slot_of(ph, rep)
            if not (isinstance(j, int) and ph.U0 + j < 2):
                sp.wait_ge(lo_made, ph.U0 + j - 1)
            sp.dma_start(raw[:, slot, 0:ph.width], dram_of[ph][j]).then_inc(raw_in[slot], 16)

        def split_hi(act, ph, j, rep):
            slot, U = slot_of(ph, rep), ph.U0 + j
            act.wait_ge(raw_in[slot], 8 * U + (16 - 8 * slot))
            if not (isinstance(j, int) and U < 2):
                act.wait_ge(unit_done, U - 1)
            nc.scalar.activation(w_hi[:, slot, 0:ph.width], raw[:, slot, 0:ph.width],
                                 ACT.Copy).then_inc(hi_made, 1)

        def split_lo(pool, ph, j, rep):
            slot = slot_of(ph, rep)
            pool.wait_ge(hi_made, ph.U0 + j + 1)
            nc.gpsimd.tensor_tensor(w_lo[:, slot, 0:ph.width], raw[:, slot, 0:ph.width],
                                    w_hi[:, slot, 0:ph.width].bitcast(F32), ALU.subtract).then_inc(lo_made, 1)

        def ahead(split, eng, ph, j, rep=None):
            if isinstance(j, int) and j >= ph.units:
                k = PH.index(ph) + 1
                if k < len(PH):
                    split(eng, PH[k], j - ph.units, j - ph.units)
            else:
                split(eng, ph, j, j if rep is None else rep)

        def wait_bank(pe, ph, j):
            if isinstance(j, int) and j < 2:
                if ph.prev is not None:
                    pv = ph.prev
                    pe.wait_ge(evac[pv.kind], pv.before[pv.kind] + pv.chunks - 1 + j)
            else:
                pe.wait_ge(evac[ph.kind], ph.before[ph.kind] + j - 1)

        def product(acc, slot, c, hi, lo, first, last):
            wh, wl = w_hi[:, slot, c * P:(c + 1) * P], w_lo[:, slot, c * P:(c + 1) * P]
            nc.tensor.matmul(acc[:], wh, hi, start=first, stop=False)
            nc.tensor.matmul(acc[:], wh, lo, start=False, stop=False)
            return nc.tensor.matmul(acc[:], wl, hi, start=False, stop=last)

        def in_unit(pe, ph, j, rep):
            pe.wait_ge(lo_made, ph.U0 + j + 1)
            wait_bank(pe, ph, j)
            for c in range(KC):
                last = product(acc_of(ph, rep), slot_of(ph, rep), c, hn_hi[:, c, :], hn_lo[:, c, :],
                               c == 0, c == KC - 1)
            last.then_inc(unit_done, 1)

        def norm_stat(parts, mean):
            for b in range(NB):
                for i, part in enumerate(parts):
                    last = nc.tensor.matmul(b_norm[:, b:b + 1], part[:, b * P:(b + 1) * P],
                                            mean_col[:, mean:mean + 1], start=i == 0, stop=i == len(parts) - 1)
            last.then_inc(stat_ready, 1)

        def norm_root(act, n):
            act.wait_ge(stat_ready, n + 1)
            nc.scalar.activation(root[:], b_norm[:, 0:NB], ACT.Sqrt, bias=eps[:]).then_inc(root_ready, 1)

        def norm_diag(dve, n):
            dve.wait_ge(root_ready, n + 1)
            if not (isinstance(n, int) and n < 1):
                dve.wait_ge(diag_ready, n)
                dve.wait_ge(bc_ready, n)
            ch(nc.vector.reciprocal(rcol[:], root[:]))
            dve.wait_ge(dve_done, ch.value())
            nc.vector.tensor_tensor(diag[:], ident[:].unsqueeze(1).to_broadcast([P, NB, P]),
                                    rcol[:].unsqueeze(2).to_broadcast([P, NB, P]),
                                    ALU.mult).then_inc(diag_ready, 1)

        def norm_bcast(pe, n):
            pe.wait_ge(diag_ready, n + 1)
            nc.tensor.matmul(b_norm[:], ones[:], diag[:].rearrange("p b t -> p (b t)"),
                             start=True, stop=True).then_inc(bc_ready, 1)

        def square(act, n, m, rep, src):
            if not (isinstance(m, int) and KC * n + m < 2):
                act.wait_ge(sq_added, KC * n + m - 1)
            return nc.scalar.activation(sq[:, rep % 2, :], src, ACT.Square)

        def add_square(pool, name, m, rep):
            n = sum_no[name]
            if isinstance(m, int) and m == 0:
                if n:
                    before = [k for k in sum_no if sum_no[k] == n - 1][0]
                    pool.wait_ge(stat_ready, norm_no[before] + 1)
            else:
                pool.wait_ge(sq_added, KC * n + m)
            pool.wait_ge(sq_ready, KC * n + m + 1)
            if isinstance(m, int) and m == 0:
                nc.gpsimd.tensor_copy(ssq[:], sq[:, 0, :]).then_inc(sq_added, 1)
            else:
                nc.gpsimd.tensor_tensor(ssq[:], ssq[:], sq[:, rep % 2, :], ALU.add).then_inc(sq_added, 1)

        GAINS = {0: (None, (0, 0)), 1: ((0, 1), (0, 2)), 2: ((0, 3), (1, 0)), 3: ((1, 1), (1, 2)), 4: ((1, 3), None)}

        def boundary_pe(pe, b, nxt=None):
            if b:
                pe.wait_ge(sq_added, KC * (sum_no[f"post{b}"] + 1))
                pe.wait_ge(rpre_copied, b)
                norm_stat([ssq], 0)
                norm_bcast(pe, norm_no[f"post{b}"])
            if nxt is None:
                return
            for j in range(2):
                pe.wait_ge(lo_made, nxt.U0 + j + 1)
                wait_bank(pe, nxt, j)
            for c in range(KC):
                pe.wait_ge(hnlo_ready, KC * b + c + 1)
                for j in range(2):
                    last = product(acc_of(nxt, j), slot_of(nxt, j), c, hn_hi[:, c, :], hn_lo[:, c, :],
                                   c == 0, c == KC - 1)
                    if c == KC - 1:
                        last.then_inc(unit_done, 1)
            pe.wait_ge(sq_added, KC * (sum_no[f"pre{b}"] + 1))
            norm_stat([ssq], 0)
            norm_bcast(pe, norm_no[f"pre{b}"])

        def boundary_act(act, b):
            if b:
                norm_root(act, norm_no[f"post{b}"])
            if GAINS[b][1] is None:
                return
            for m in range(KC):
                if b:
                    act.wait_ge(x_new, KC * (b - 1) + m + 1)
                nc.scalar.activation(hn_hi[:, m, :], x[:, m, :], ACT.Copy,
                                     scale=gain(*GAINS[b][1], m)).then_inc(hnhi_ready, 1)
                square(act, sum_no[f"pre{b}"], m, m, x[:, m, :]).then_inc(sq_ready, 1)
            norm_root(act, norm_no[f"pre{b}"])
            act.wait_ge(bc_ready, norm_no[f"pre{b}"] + 1)
            nc.scalar.activation(r_pre[:], b_norm[:], ACT.Copy).then_inc(rpre_copied, 1)

        def boundary_pool(pool, b):
            if GAINS[b][1] is not None:
                for m in range(KC):
                    add_square(pool, f"pre{b}", m, m)

        def boundary_dve(dve, b):
            def lo(m):
                dve.wait_ge(hnhi_ready, KC * b + m + 1)
                nc.vector.scalar_tensor_tensor(hn_lo[:, m, :], x[:, m, :], gain(*GAINS[b][1], m),
                                               hn_hi[:, m, :].bitcast(F32), ALU.mult, ALU.subtract
                                               ).then_inc(hnlo_ready, 1)

            if b:
                norm_diag(dve, norm_no[f"post{b}"])
                dve.wait_ge(bc_ready, norm_no[f"post{b}"] + 1)
            for m in range(KC):
                if b:
                    ch(nc.vector.scalar_tensor_tensor(mbuf[:, m, :], mbuf[:, m, :], gain(*GAINS[b][0], m),
                                                      b_norm[:], ALU.mult, ALU.mult))
                    dve.wait_ge(dve_done, ch.value())
                    nc.vector.tensor_tensor(x[:, m, :], x[:, m, :], mbuf[:, m, :], ALU.add).then_inc(x_new, 1)
                if m and GAINS[b][1] is not None:
                    lo(m - 1)
            if GAINS[b][1] is not None:
                lo(KC - 1)
                norm_diag(dve, norm_no[f"pre{b}"])
                dve.wait_ge(rpre_copied, b + 1)

        def out_halves_pe(pe, ph, i, hi, lo, tiles, ready=None, mid=None):
            for q in range(4):
                half, s = divmod(q, 2)
                pe.wait_ge(lo_made, ph.U0 + 4 * i + q + 1)
                if half == 0:
                    wait_bank(pe, ph, 2 * i + s)
                for c in range(tiles):
                    k = half * tiles + c
                    if ready is not None and s == 0:
                        ready(k)
                    last = product(acc_of(ph, s), slot_of(ph, q), c, hi[:, k, :], lo[:, k, :],
                                   k == 0, k == 2 * tiles - 1)
                last.then_inc(unit_done, 1)
                if mid is not None:
                    mid(q)

        def out_chunk_act(act, ph, m, rep, b, units_before):
            act.wait_ge(unit_done, ph.U0 + units_before)
            acc = acc_of(ph, rep)
            square(act, sum_no[f"post{b}"], m, rep, acc[:]).then_inc(sq_ready, 1)
            nc.scalar.activation(mbuf[:, m, :], acc[:], ACT.Copy).then_inc(evac["out"], 1)

        def out_halves(eng, ph, i, first, split, chunk):
            if not first:
                ahead(split, eng, ph, 4 * i + 1, 1)
            ahead(split, eng, ph, 4 * i + 2, 2)
            ahead(split, eng, ph, 4 * i + 3, 3)
            chunk(2 * i, 0, 4 * i + 3)
            ahead(split, eng, ph, 4 * i + 4, 4)
            chunk(2 * i + 1, 1, 4 * i + 4)

        def out_wholes(eng, ph, i, first, split, chunk):
            if not first:
                ahead(split, eng, ph, 2 * i + 1, 1)
            chunk(2 * i, 0, 2 * i + 1)
            ahead(split, eng, ph, 2 * i + 2, 2)
            chunk(2 * i + 1, 1, 2 * i + 2)

        def out_phase(eng, ph, body, split, chunk):
            n = KC // 2
            body(eng, ph, 0, True, split, chunk)
            with eng.Fori(1, n - 1) as i:
                body(eng, ph, i, False, split, chunk)
            body(eng, ph, n - 1, False, split, chunk)
            ahead(split, eng, ph, ph.units + 1)

        def out_phase_act(act, ph, body, b):
            out_phase(act, ph, body, split_hi, lambda m, rep, u: out_chunk_act(act, ph, m, rep, b, u))
            boundary_act(act, b)

        def out_phase_pool(pool, ph, body, b):
            out_phase(pool, ph, body, split_lo, lambda m, rep, u: add_square(pool, f"post{b}", m, rep))
            boundary_pool(pool, b)

        def conv(dve, ph, j, rep, ug, taps, wcol, dst, n_conv):
            dve.wait_ge(unit_done, ph.U0 + j + 1)
            if not (isinstance(n_conv, int) and n_conv == 0):
                dve.wait_ge(conv_ready, n_conv)
            nc.vector.tensor_tensor(ug[:, taps - 1:taps - 1 + S], acc_of(ph, rep)[:], r_pre[:],
                                    ALU.mult).then_inc(evac["in"], 1)
            dve.wait_ge(evac["in"], ph.before["in"] + j + 1)
            ch(nc.vector.tensor_scalar(dst, ug[:, taps - 1:taps - 1 + S], col(wcol + taps - 1), col(wcol + taps),
                                       ALU.mult, ALU.add))
            for t in range(taps - 1):
                dve.wait_ge(dve_done, ch.value())
                ins = nc.vector.scalar_tensor_tensor(dst, ug[:, t:t + S], col(wcol + t), dst, ALU.mult, ALU.add)
                if t < taps - 2:
                    ch(ins)
            ins.then_inc(conv_ready, 1)

        def mix_y_pe(pe, g):
            pe.wait_ge(m_ready, g)
            pe.wait_ge(cs_ready, g)
            pe.wait_ge(prev_ready, g)
            for jj in range(2):
                for c in range(NB):
                    for half in range(2):
                        hh = 2 * jj + half
                        dst = b_y[HD * half:HD * half + HD, jj, c * P:(c + 1) * P]
                        last = nc.tensor.matmul(dst, xdt[:, c, hh, :], m_t[:, hh, c * P:(c + 1) * P],
                                                start=True, stop=c == 0)
                        if c:
                            last = nc.tensor.matmul(dst, prev[:, c - 1, hh, :],
                                                    cs_t[:, hh, (c - 1) * P:c * P], start=False, stop=True)
            last.then_inc(y_ready, 1)

        def mix_pe(pe, g, skip_x0=False, before=True):
            if not skip_x0:
                in_unit(pe, MIX, 1 + 6 * g, 1)
            if before:
                mix_y_pe(pe, g)
            in_unit(pe, MIX, 2 + 6 * g, 2)
            if before:
                pe.wait_ge(ysq_ready, 2 * g)
                pe.wait_ge(btok_ready, g)
                norm_stat([yt[:, 0, :], yt[:, 1, :]], 1)
            in_unit(pe, MIX, 3 + 6 * g, 3)
            if skip_x0:
                pe.wait_ge(acs_ready, 1)
                for i, src in enumerate((d_acs, d_dt)):
                    for c in range(NB):
                        last = nc.tensor.transpose(b_cb[:, (i * NB + c) * HS:(i * NB + c + 1) * HS],
                                                   src[:, c * P:(c + 1) * P], ident[0:HS, 0:HS])
                last.then_inc(dtr_ready, 1)
            in_unit(pe, MIX, 4 + 6 * g, 4)
            if skip_x0:
                pe.wait_ge(tok_ready, 1)
                nc.tensor.matmul(b_cb[:, 0:NB * HS], last_row[:], acs_tok[:].rearrange("p c h -> p (c h)"),
                                 start=True, stop=True).then_inc(tot_ready, 1)
            if before:
                norm_bcast(pe, norm_no["group"] + g - 1)
            in_unit(pe, MIX, 5 + 6 * g, 5)
            pe.wait_ge(silu_ready, 6 * g + 4)
            if before:
                pe.wait_ge(y_normed, 2 * g)
            else:
                pe.wait_ge(rpre_copied, 1)
            for c in range(NB):
                last = nc.tensor.transpose(b_norm[:, c * P:(c + 1) * P], bT[:, c * P:(c + 1) * P], ident[:])
            last.then_inc(trb_ready, 1)
            if before:
                pe.wait_ge(prev_ready, g)
            for c in range(NB):
                for jj in range(2):
                    at_c = (c % 2) * 2 * P + jj * P
                    last = nc.tensor.transpose(b_x[:, c // 2, at_c:at_c + P], xc[:, jj, c * P:(c + 1) * P], ident[:])
            last.then_inc(trx_ready, 1)
            if before:
                pe.wait_ge(cbm_ready, g)
            else:
                pe.wait_ge(dec_in, 1)
            for c in range(NB):
                last = nc.tensor.matmul(b_cb[:, c * P:(c + 1) * P], bT[:, c * P:(c + 1) * P],
                                        cT[:, c * P:(c + 1) * P], start=True, stop=True)
            last.then_inc(cb_ready, 1)
            in_unit(pe, MIX, 6 + 6 * g, 6)
            pe.wait_ge(xw_ready, g + 1)
            pe.wait_ge(btok_ready, g + 1)
            for c in range(NB - 1):
                last = nc.tensor.matmul(b_x[:, c // 2, (c % 2) * 2 * P:(c % 2) * 2 * P + 2 * P], btok[:, c, :],
                                        xdd[:, c, :, :].rearrange("p h d -> p (h d)"), start=True, stop=True)
            last.then_inc(st_ready, 1)

        def mix_act(act, g, first=False, proj=True, before=True):
            def silu(dst, src):
                nc.scalar.activation(dst, src, ACT.Silu).then_inc(silu_ready, 1)

            if proj:
                ahead(split_hi, act, MIX, 2 + 6 * g, 2)
                act.wait_ge(conv_ready, 4 * g + 1)
                if before:
                    act.wait_ge(trx_ready, g)
                silu(xc[:, 0, :], cv_s[:])
                if first:
                    act.wait_ge(dt_in, 1)
                    nc.scalar.activation(d_e[:], d_w[:], ACT.Exp).then_inc(dt_exp, 1)
                    nc.scalar.activation(d_ea[:], par[0:HS, ALOG:ALOG + 1], ACT.Exp).then_inc(al_exp, 1)
                    act.wait_ge(acs_ready, 1)
                    nc.scalar.activation(d_z[:], d_acs[:], ACT.Exp).then_inc(ecs_ready, 1)
                ahead(split_hi, act, MIX, 3 + 6 * g, 3)
                act.wait_ge(conv_ready, 4 * g + 2)
                silu(xc[:, 1, :], cv_s[:])
            if before:
                for jj in range(2):
                    act.wait_ge(y_gated, 2 * g - 1 + jj)
                    nc.scalar.activation(yt[:, jj, :], y_at(2 * g - 2 + jj), ACT.Square).then_inc(ysq_ready, 1)
            if proj:
                ahead(split_hi, act, MIX, 4 + 6 * g, 4)
                act.wait_ge(conv_ready, 4 * g + 3)
                if before:
                    act.wait_ge(cb_ready, g)
                silu(bT[:], cv_s[:])
            if before:
                norm_root(act, norm_no["group"] + g - 1)
            if not proj:
                return
            ahead(split_hi, act, MIX, 5 + 6 * g, 5)
            act.wait_ge(conv_ready, 4 * g + 4)
            if before:
                act.wait_ge(cs_ready, g)
            silu(cT[:], cv_s[:])
            if first:
                act.wait_ge(dec_in, 1)
                nc.scalar.activation(wdec[:], wdec[:], ACT.Exp).then_inc(dec_exp, 1)
            act.wait_ge(silu_ready, 6 * g + 2)
            for jj in range(2):
                nc.scalar.activation(yt[:, jj, :], xc[:, jj, :], ACT.Copy,
                                     scale=col(SSM0 + SSMW * g + 4 * (SSM_T + 1) + jj)).then_inc(skip_ready, 1)
            ahead(split_hi, act, MIX, 6 + 6 * g, 6)
            act.wait_ge(evac["in"], 6 * g + 6)
            silu(zs[:, 0, :], zs[:, 0, :])
            act.wait_ge(trb_ready, g + 1)
            if before:
                act.wait_ge(st_ready, g)
            nc.scalar.activation(btok[:].rearrange("p c n -> p (c n)"), b_norm[:], ACT.Copy).then_inc(btok_ready, 1)
            act.wait_ge(seg_ready, g + 1)
            nc.scalar.activation(m_t[:], m_t[:], ACT.Exp).then_inc(seg_exp, 1)
            ahead(split_hi, act, MIX, 7 + 6 * g, 7)
            act.wait_ge(evac["in"], 6 * g + 7)
            silu(zs[:, 1, :], zs[:, 1, :])

        def mix_pool(pool, g, first=False):
            for c in range(6):
                ahead(split_lo, pool, MIX, 2 + c + 6 * g, 2 + c)
                if c == 4:
                    pool.wait_ge(silu_ready, 6 * g + 4)
                    pool.wait_ge(ecs_in, 16 * g + 16)
                    if not first:
                        pool.wait_ge(y_ready, g)
                    nc.gpsimd.tensor_tensor(cs_t[:], cT[:, P:S].unsqueeze(1).to_broadcast([P, HG, S - P]),
                                            ecs_bc[:, :, P:S], ALU.mult).then_inc(cs_ready, 1)

        def y_at(k):
            return ybuf[:, k, :]

        def mix_conv(dve, g, c, first):
            if not (first and c == 0):
                dve.wait_ge(silu_ready, 6 * g + c if c else 6 * g - 2)
            conv(dve, MIX, 1 + 6 * g + c, 1 + c, ug_s, SSM_T, SSM0 + SSMW * g + (SSM_T + 1) * c, cv_s[:], 4 * g + c)

        def y_gate_dve(dve, g):
            dve.wait_ge(y_ready, g)
            dve.wait_ge(skip_ready, 2 * g)
            dve.wait_ge(silu_ready, 6 * g)
            for jj in range(2):
                ch(nc.vector.tensor_tensor(yt[:, jj, :], b_y[:, jj, :], yt[:, jj, :], ALU.add))
            for jj in range(2):
                dve.wait_ge(dve_done, ch.value() - 1 + jj)
                nc.vector.tensor_tensor(y_at(2 * g - 2 + jj), yt[:, jj, :], zs[:, jj, :], ALU.mult).then_inc(y_gated, 1)

        def y_norm_dve(dve, g):
            dve.wait_ge(bc_ready, norm_no["group"] + g)
            dve.wait_ge(y_gated, 2 * g)
            dve.wait_ge(ysq_ready, 2 * g)
            for jj in range(2):
                nc.vector.scalar_tensor_tensor(
                    y_at(2 * g - 2 + jj), y_at(2 * g - 2 + jj),
                    col(SSM0 + SSMW * (g - 1) + 4 * (SSM_T + 1) + 2 + jj), b_norm[:],
                    ALU.mult, ALU.mult).then_inc(y_normed, 1)

        def dt_dve(dve):
            def step(ins):
                ch(ins)
                dve.wait_ge(dve_done, ch.value())

            step(nc.vector.tensor_scalar(d_v[:], d_v[:], par[0:HS, DTB:DTB + 1], None, ALU.add))
            nc.vector.scalar_tensor_tensor(d_w[:], d_v[:], -1.0, d_v[:], ALU.mult, ALU.min).then_inc(dt_in, 1)
            dve.wait_ge(dt_exp, 1)
            step(nc.vector.tensor_scalar(d_p[:], d_e[:], 2.0, None, ALU.add))
            step(nc.vector.reciprocal(d_p[:], d_p[:]))
            step(nc.vector.tensor_tensor(d_z[:], d_e[:], d_p[:], ALU.mult))
            step(nc.vector.tensor_tensor(d_w[:], d_z[:], d_z[:], ALU.mult))
            step(nc.vector.tensor_scalar(d_p[:], d_w[:], 1.0 / 15, None, ALU.mult))
            for k in (13, 11, 9, 7, 5, 3):
                step(nc.vector.scalar_tensor_tensor(d_p[:], d_p[:], 1.0 / k, d_w[:], ALU.add, ALU.mult))
            step(nc.vector.scalar_tensor_tensor(d_p[:], d_p[:], 1.0, d_z[:], ALU.add, ALU.mult))
            step(nc.vector.tensor_scalar(d_v[:], d_v[:], 0.0, None, ALU.max))
            step(nc.vector.scalar_tensor_tensor(d_dt[:], d_p[:], 2.0, d_v[:], ALU.mult, ALU.add))
            dve.wait_ge(al_exp, 1)
            step(nc.vector.tensor_scalar(d_e[:], d_dt[:], d_ea[:], -1.0, ALU.mult, ALU.mult))
            for c in range(NB):
                ins = nc.vector.tensor_tensor_scan(d_acs[:, c * P:(c + 1) * P], ones[0:HS, :],
                                                   d_e[:, c * P:(c + 1) * P], 0.0, ALU.mult, ALU.add)
            ins.then_inc(acs_ready, 1)

        def mix_dve(dve, g, first=False, proj=True, before=True, mid=None):
            if proj:
                mix_conv(dve, g, 0, first)
                if first:
                    dt_dve(dve)
                mix_conv(dve, g, 1, first)
            if before:
                y_gate_dve(dve, g)
            if proj:
                mix_conv(dve, g, 2, first)
                if first:
                    dve.wait_ge(dtr_ready, 1)
                    ch(nc.vector.tensor_copy(dt_tok[:].rearrange("p c h -> p (c h)"), b_cb[:, NB * HS:2 * NB * HS]))
                    ch(nc.vector.tensor_scalar(nacs[:].rearrange("p c h -> p (c h)"), b_cb[:, 0:NB * HS],
                                               -1.0, None, ALU.mult))
                    nc.vector.tensor_copy(acs_tok[:].rearrange("p c h -> p (c h)"),
                                          b_cb[:, 0:NB * HS]).then_inc(tok_ready, 1)
            if before:
                norm_diag(dve, norm_no["group"] + g - 1)
            if proj:
                mix_conv(dve, g, 3, first)
                if first:
                    dve.wait_ge(tot_ready, 1)
                    dve.wait_ge(dve_done, ch.value())
                    nc.vector.tensor_tensor(wdec[:].rearrange("p c h -> p (c h)"), b_cb[:, 0:NB * HS],
                                            nacs[:].rearrange("p c h -> p (c h)"), ALU.add).then_inc(dec_in, 1)
                    dve.wait_ge(dec_exp, 1)
                    ch(nc.vector.tensor_tensor(wdec[:], wdec[:], dt_tok[:], ALU.mult))
                    dve.wait_ge(dve_done, ch.value())
            if before:
                y_norm_dve(dve, g)
            if not proj:
                return
            dve.wait_ge(unit_done, 6 * g + 6)
            nc.vector.tensor_tensor(zs[:, 0, :], acc_of(MIX, 5)[:], r_pre[:], ALU.mult).then_inc(evac["in"], 1)
            if not first:
                dve.wait_ge(seg_ready, g)
            ch(nc.vector.tensor_copy(nac_g[:], nacs[:, :, bass.ds(HG * g, HG)]))
            dve.wait_ge(dve_done, ch.value())
            dve.wait_ge(acs_in, 16 * g + 16)
            if not first:
                dve.wait_ge(y_ready, g)
            for hh in range(HG):
                for c in range(NB):
                    ins = nc.vector.tensor_scalar(m_t[:, hh, c * P:(c + 1) * P], acs_bc[:, hh, c * P:(c + 1) * P],
                                                  nac_g[:, c, hh:hh + 1], 0.0, ALU.add, ALU.min)
            ins.then_inc(seg_ready, 1)
            dve.wait_ge(trx_ready, g + 1)
            if not first:
                dve.wait_ge(st_ready, g)
            for wgt, dst in ((dt_tok, xdt), (wdec, xdd)):
                for half in range(2):
                    ins = nc.vector.tensor_tensor(
                        dst[:, 2 * half:2 * half + 2, :, :],
                        b_x[:, half, :].rearrange("p (c h d) -> p c h d", c=2, h=HG),
                        wgt[:, 2 * half:2 * half + 2, bass.ds(HG * g, HG)].unsqueeze(3).to_broadcast([P, 2, HG, HD]),
                        ALU.mult)
            ins.then_inc(xw_ready, 1)
            dve.wait_ge(cb_ready, g + 1)
            if not first:
                dve.wait_ge(m_ready, g)
            nc.vector.tensor_tensor(cbm[:].rearrange("p (c l) -> p c l", c=NB),
                                    b_cb[:].rearrange("p (c l) -> p c l", c=NB),
                                    tri[:].unsqueeze(1).to_broadcast([P, NB, P]), ALU.mult).then_inc(cbm_ready, 1)
            dve.wait_ge(unit_done, 6 * g + 7)
            nc.vector.tensor_tensor(zs[:, 1, :], acc_of(MIX, 6)[:], r_pre[:], ALU.mult).then_inc(evac["in"], 1)
            dve.wait_ge(st_ready, g + 1)
            dve.wait_ge(ecs_in, 16 * g + 16)
            if not first:
                dve.wait_ge(prev_ready, g)

            def st(c):
                return b_x[:, c // 2, (c % 2) * 2 * P:(c % 2) * 2 * P + 2 * P].rearrange("p (h d) -> p h d", h=HG)

            ch(nc.vector.tensor_copy(prev[:, 0, :, :], st(0)))
            for c in range(1, NB - 1):
                dve.wait_ge(dve_done, ch.value())
                ch(nc.vector.tensor_tensor(
                    pdec[:], prev[:, c - 1, :, :],
                    ecs_bc[:, :, (c + 1) * P - 1:(c + 1) * P].to_broadcast([P, HG, HD]), ALU.mult))
                dve.wait_ge(dve_done, ch.value())
                ins = nc.vector.tensor_tensor(prev[:, c, :, :], pdec[:], st(c), ALU.add)
                if c < NB - 2:
                    ch(ins)
            ins.then_inc(prev_ready, 1)
            dve.wait_ge(seg_exp, g + 1)
            dve.wait_ge(cbm_ready, g + 1)
            nc.vector.tensor_tensor(m_t[:], m_t[:], cbm[:].unsqueeze(1).to_broadcast([P, HG, S]),
                                    ALU.mult).then_inc(m_ready, 1)

        def y_split_act(act, ks):
            for k in ks:
                nc.scalar.activation(y_hi[:, k, :], y_at(k), ACT.Copy).then_inc(yhi_ready, 1)

        def y_split_dve(dve, ks):
            for k in ks:
                dve.wait_ge(yhi_ready, k + 1)
                nc.vector.tensor_tensor(y_lo[:, k, :], y_at(k), y_hi[:, k, :].bitcast(F32),
                                        ALU.subtract).then_inc(ylo_ready, 1)

        def ffn_pe(pe, up, dn, layer):
            with pe.Fori(1, FC) as m:
                in_unit(pe, up, 2 * m, 0)
                in_unit(pe, up, 2 * m + 1, 1)
            out_halves_pe(pe, dn, 0, h_hi, h_lo, HU, ready=lambda k: pe.wait_ge(hlo_ready, layer * FC + k + 1))
            with pe.Fori(1, KC // 2) as i:
                out_halves_pe(pe, dn, i, h_hi, h_lo, HU)

        def ffn_act(act, up, layer):
            def hidden_hi(m):
                act.wait_ge(hb_ready, layer * FC + m + 1)
                nc.scalar.activation(h_hi[:, m, :], hb[:], ACT.Copy).then_inc(hhi_ready, 1)

            def pair(m, first=False):
                if not first:
                    ahead(split_hi, act, up, 2 * m + 1, 1)
                    hidden_hi(m - 1)
                act.wait_ge(conv_ready, 4 * NG + layer * 2 * FC + 2 * m + 1)
                if not (first and layer == 0):
                    act.wait_ge(hb_ready, layer * FC + m)
                nc.scalar.activation(sg[:], cg[:], ACT.Silu).then_inc(gate_ready, 1)
                ahead(split_hi, act, up, 2 * m + 2, 2)

            pair(0, True)
            with act.Fori(1, FC - 1) as m:
                pair(m)
            pair(FC - 1)
            hidden_hi(FC - 1)
            ahead(split_hi, act, up, up.units + 1)

        def ffn_pool(pool, up):
            ahead(split_lo, pool, up, 2, 2)
            with pool.Fori(1, FC - 1) as m:
                ahead(split_lo, pool, up, 2 * m + 1, 1)
                ahead(split_lo, pool, up, 2 * m + 2, 2)
            ahead(split_lo, pool, up, up.units - 1)
            ahead(split_lo, pool, up, up.units)
            ahead(split_lo, pool, up, up.units + 1)

        def ffn_dve(dve, up, layer):
            base = layer * FC

            def hidden_lo(m):
                dve.wait_ge(hhi_ready, base + m + 1)
                nc.vector.tensor_tensor(h_lo[:, m, :], hb[:], h_hi[:, m, :].bitcast(F32),
                                        ALU.subtract).then_inc(hlo_ready, 1)

            def pair(m, first=False):
                n_conv = 4 * NG + 2 * base + 2 * m
                w = FFN0 + FFNW * base + FFNW * m
                if not (first and layer == 0):
                    dve.wait_ge(gate_ready, base + m)
                conv(dve, up, 2 * m, 0, ug_f, FFN_T, w, cg[:], n_conv)
                if not first:
                    hidden_lo(m - 1)
                if not (first and layer == 0):
                    dve.wait_ge(hb_ready, base + m)
                conv(dve, up, 2 * m + 1, 1, ug_f, FFN_T, w + FFN_T + 1, cu[:], n_conv + 1)
                dve.wait_ge(conv_ready, n_conv + 2)
                dve.wait_ge(gate_ready, base + m + 1)
                if not (first and layer == 0):
                    dve.wait_ge(hlo_ready, base + m)
                nc.vector.tensor_tensor(hb[:], sg[:], cu[:], ALU.mult).then_inc(hb_ready, 1)

            memzero = nc.vector.memset(ug_f[:, 0:FFN_T - 1], 0.0)
            ch(memzero)
            dve.wait_ge(dve_done, ch.value())
            pair(0, True)
            with dve.Fori(1, FC) as m, ch.loop(m, 1, FC - 1, 2 * (FFN_T - 1)):
                pair(m)
            hidden_lo(FC - 1)

        def use(h, name):
            if isinstance(h, int) and h == 1:
                return {"v": 0, "t0": 1, "t1": 2}[name]
            if isinstance(h, int) and h == NH + 1:
                return 3 + 5 * (NH - 1) + {"t2": 0, "t3": 1}[name]
            return 5 * h + (3 - 10) + {"v": 0, "t2": 1, "t3": 2, "t0": 3, "t1": 4}[name]

        def att_pe(pe, h, b):
            proj = not (isinstance(h, int) and h >= NH)
            one = not (isinstance(h, int) and not 1 <= h <= NH)
            two = not (isinstance(h, int) and h < 2)
            rep = 3 * b
            b1, b2 = 1 - b, b

            def bank_free(name):
                n = use(h, name)
                if not (isinstance(n, int) and n == 0):
                    pe.wait_ge(tr_copied, n)

            def scores(i):
                n, keys = 4 * (h - 1) + i, (i + 1) * P
                if not (isinstance(n, int) and n < 2):
                    pe.wait_ge(s_taken, n - 1)
                for t in range(2):
                    last = nc.tensor.matmul(scores_in[i % 2][:, t, 0:keys],
                                            qT[DH * t:DH * t + DH, b1, i * P:(i + 1) * P],
                                            kT[DH * t:DH * t + DH, b1, 0:keys], start=True, stop=True)
                last.then_inc(s_ready, 1)

            def weights_back(i, name, a):
                bank_free(name)
                pe.wait_ge(a_ready, 4 * a + i + 1)
                for jb in range(i + 1):
                    last = nc.tensor.transpose(b_tr[:, jb * P:(jb + 1) * P], at[:, i % 2, jb * P:(jb + 1) * P],
                                               ident[:])
                last.then_inc(tr_ready, 1)

            if proj and not (isinstance(h, int) and h == 0):
                in_unit(pe, QKV, 3 * h, rep)
            if one:
                bank_free("v")
                pe.wait_ge(evac["in"], QKV.before["in"] + 3 * h)
                for c in range(NB):
                    last = nc.tensor.transpose(b_tr[:, c * P:(c + 1) * P], vT[:, b1, c * P:(c + 1) * P], ident[:])
                last.then_inc(tr_ready, 1)
                scores(0)
                scores(1)
            if two:
                weights_back(2, "t2", h - 2)
                weights_back(3, "t3", h - 2)
                pe.wait_ge(tr_copied, use(h, "t3") + 1)
                for jb in range(NB):
                    last = nc.tensor.matmul(b_pv[:, jb * P:S], vtok[:, b2, jb, :], aT[:, jb, jb * P:S],
                                            start=jb == 0, stop=jb == NB - 1)
                last.then_inc(pv_ready, 1)
            if proj and not (isinstance(h, int) and h == 0):
                in_unit(pe, QKV, 3 * h + 1, rep + 1)
            if one:
                weights_back(0, "t0", h - 1)
                scores(2)
                scores(3)
            if two:
                pe.wait_ge(ob_ready, h - 1)
                norm_stat([osq], 2)
            if proj:
                in_unit(pe, QKV, 3 * h + 2, rep + 2)
            if one:
                weights_back(1, "t1", h - 1)
            if two:
                norm_bcast(pe, norm_no["head"] + h - 2)

        def att_act(act, h, b):
            proj = not (isinstance(h, int) and h >= NH)
            one = not (isinstance(h, int) and not 1 <= h <= NH)
            two = not (isinstance(h, int) and h < 2)
            first = isinstance(h, int) and h == 0
            rep = 3 * b
            b1 = 1 - b

            def probs(i):
                n, keys, sl = 4 * (h - 1) + i, (i + 1) * P, i % 2
                act.wait_ge(mx_ready, n + 1)
                if not (isinstance(n, int) and n < 2):
                    act.wait_ge(a_ready, n - 1)
                for t in range(2):
                    ins = nc.scalar.activation(pr[:, sl, t, 0:keys], sc[:, sl, t, 0:keys], ACT.Exp,
                                               bias=nmx[:, sl, t:t + 1], accum_out=den[:, sl, t:t + 1])
                ins.then_inc(p_ready, 1)

            def copy_back(i, name, a):
                act.wait_ge(tr_ready, use(h, name) + 1)
                if name == "t0" and not (isinstance(a, int) and a == 0):
                    act.wait_ge(pv_ready, a)
                nc.scalar.activation(aT[:, 0:i + 1, i * P:(i + 1) * P],
                                     b_tr[:, 0:(i + 1) * P].rearrange("p (j q) -> p j q", j=i + 1),
                                     ACT.Copy).then_inc(tr_copied, 1)

            if proj and not first:
                ahead(split_hi, act, QKV, 3 * h + 1, rep + 1)
            if one:
                act.wait_ge(tr_ready, use(h, "v") + 1)
                nc.scalar.activation(vtok[:, b1, :, :].rearrange("p c e -> p (c e)"), b_tr[:],
                                     ACT.Copy).then_inc(tr_copied, 1)
                probs(0)
                probs(1)
            if two:
                copy_back(2, "t2", h - 2)
                copy_back(3, "t3", h - 2)
            if proj:
                ahead(split_hi, act, QKV, 3 * h + 2, rep + 2)
            if two:
                act.wait_ge(pv_ready, h - 1)
                nc.scalar.activation(ob[:], b_pv[:], ACT.Copy)
                nc.scalar.activation(osq[:], b_pv[:], ACT.Square).then_inc(ob_ready, 1)
            if one:
                copy_back(0, "t0", h - 1)
                probs(2)
                probs(3)
            if two:
                norm_root(act, norm_no["head"] + h - 2)
            if proj:
                ahead(split_hi, act, QKV, 3 * h + 3, rep + 3)
            if one:
                copy_back(1, "t1", h - 1)
            if two:
                act.wait_ge(on_ready, h - 1)
                nc.scalar.activation(o_hi[:, h - 2, :], on[:], ACT.Copy).then_inc(ohi_ready, 1)

        def att_dve(dve, h, b):
            proj = not (isinstance(h, int) and h >= NH)
            one = not (isinstance(h, int) and not 1 <= h <= NH)
            two = not (isinstance(h, int) and h < 2)
            rep = 3 * b

            def take(j, dst):
                dve.wait_ge(unit_done, QKV.U0 + 3 * h + j + 1)
                if dst is qT:
                    ins = nc.vector.scalar_tensor_tensor(dst[:, b, :], acc_of(QKV, rep + j)[:], DH ** -0.5,
                                                         r_pre[:], ALU.mult, ALU.mult)
                else:
                    ins = nc.vector.tensor_tensor(dst[:, b, :], acc_of(QKV, rep + j)[:], r_pre[:], ALU.mult)
                ins.then_inc(evac["in"], 1)

            def biased(i):
                n, keys, sl = 4 * (h - 1) + i, (i + 1) * P, i % 2
                dve.wait_ge(s_ready, n + 1)
                if not (isinstance(n, int) and n < 2):
                    dve.wait_ge(p_ready, n - 1)
                nc.vector.scalar_tensor_tensor(
                    sc[:, sl, :, 0:keys], dist[:, S - keys:S].unsqueeze(1).to_broadcast([P, 2, keys]),
                    slopes[:, bass.ds(h - 1, 1)], scores_in[sl][:, :, 0:keys], ALU.mult, ALU.add).then_inc(s_taken, 1)
                dve.wait_ge(s_taken, n + 1)
                nc.vector.tensor_reduce(nmx[:, sl, :], sc[:, sl, :, 0:keys], AX.X, ALU.max,
                                        negate=True).then_inc(mx_ready, 1)

            def combine(i):
                n, keys, sl = 4 * (h - 1) + i, (i + 1) * P, i % 2
                dve.wait_ge(p_ready, n + 1)
                if not (isinstance(n, int) and n < 2):
                    dve.wait_ge(a_ready, n - 1)
                    dve.wait_ge(tr_ready, at_used(i))
                ch(nc.vector.reciprocal(cf[:, sl, :], den[:, sl, :]))
                dve.wait_ge(dve_done, ch.value())
                ch(nc.vector.tensor_scalar(cf[:, sl, 1:2], cf[:, sl, 1:2], lam_s[:, 4:5], None, ALU.mult))
                ch(nc.vector.tensor_scalar(at[:, sl, 0:keys], pr[:, sl, 0, 0:keys], cf[:, sl, 0:1], None, ALU.mult))
                dve.wait_ge(dve_done, ch.value())
                nc.vector.scalar_tensor_tensor(at[:, sl, 0:keys], pr[:, sl, 1, 0:keys], cf[:, sl, 1:2],
                                               at[:, sl, 0:keys], ALU.mult, ALU.add).then_inc(a_ready, 1)

            def at_used(i):
                return {0: lambda: use(h, "t2") + 1, 1: lambda: use(h, "t3") + 1,
                        2: lambda: use(h, "t0") + 1, 3: lambda: use(h, "t1") + 1}[i]()

            if proj:
                take(0, qT)
            if one:
                biased(0)
                biased(1)
                combine(0)
            if proj:
                take(1, kT)
            if one:
                combine(1)
                biased(2)
                biased(3)
                combine(2)
            if two:
                norm_diag(dve, norm_no["head"] + h - 2)
            if proj:
                take(2, vT)
            if one:
                combine(3)
            if two:
                dve.wait_ge(bc_ready, norm_no["head"] + h - 1)
                nc.vector.scalar_tensor_tensor(on[:], ob[:], gsub[:], b_norm[:], ALU.mult,
                                               ALU.mult).then_inc(on_ready, 1)
                dve.wait_ge(ohi_ready, h - 1)
                nc.vector.tensor_tensor(o_lo[:, h - 2, :], on[:], o_hi[:, h - 2, :].bitcast(F32),
                                        ALU.subtract).then_inc(olo_ready, 1)
                dve.wait_ge(olo_ready, h - 1)

        def att_rounds(eng, part, chained=None):
            part(eng, 0, 0)
            part(eng, 1, 1)
            with eng.Fori(1, NH // 2) as i:
                if chained is None:
                    part(eng, 2 * i, 0)
                    part(eng, 2 * i + 1, 1)
                else:
                    with ch.loop(i, 1, NH // 2 - 1, chained):
                        part(eng, 2 * i, 0)
                        part(eng, 2 * i + 1, 1)
            part(eng, NH, 0)
            part(eng, NH + 1, 1)

        block = ctx.enter_context(nc.Block())

        @block.sync
        def _(sp):
            sp.dma_start(x[:], x_in).then_inc(x_in_s, 16)
            sp.dma_start(par[:], params).then_inc(par_in, 16)
            load_unit(sp, MIX, 0, 0)
            load_unit(sp, MIX, 1, 1)
            sp.dma_start(lam_v[:], lam_in.partition_broadcast(P)).then_inc(lam_in_s, 16)

            def group(g, first=False):
                for c in range(6):
                    if c == 4:
                        if first:
                            sp.wait_ge(acs_ready, 1)
                            sp.dma_start(scratch[0], d_acs[:]).then_inc(acs_out, 16)
                            sp.wait_ge(ecs_ready, 1)
                            sp.dma_start(scratch[1], d_z[:]).then_inc(ecs_out, 16)
                            sp.wait_ge(acs_out, 16)
                            sp.wait_ge(ecs_out, 16)
                        else:
                            sp.wait_ge(seg_ready, g)
                            sp.wait_ge(prev_ready, g)
                            sp.wait_ge(cs_ready, g)
                        for k, (dst, done) in enumerate(((acs_bc, acs_in), (ecs_bc, ecs_in))):
                            rows = scratch[k, bass.ds(HG * g, HG), :]
                            sp.dma_start(dst[:], rows.partition_broadcast(P)).then_inc(done, 16)
                    if c or not first:
                        load_unit(sp, MIX, 1 + 6 * g + c, 1 + c)

            group(0, True)
            with sp.Fori(1, NG) as g:
                group(g)
            for ph in PH[1:]:
                with sp.Fori(0, ph.units // 2) as i:
                    load_unit(sp, ph, 2 * i, 0)
                    load_unit(sp, ph, 2 * i + 1, 1)
            for m in range(KC):
                sp.wait_ge(x_new, 3 * KC + m + 1)
                sp.dma_start(out[:, m, :], x[:, m, :]).then_inc(y_sent, 16)
            sp.wait_ge(y_sent, 16 * KC)

        @block.gpsimd
        def _(pool):
            n = 0

            def const(ins):
                nonlocal n
                ins.then_inc(consts, 1)
                n += 1

            def picked(tile, base, step, cmp, fill, width=P):
                pool.wait_ge(consts, n)
                const(nc.gpsimd.affine_select(out=tile, in_=tile, compare_op=cmp, fill=fill, base=base,
                                              pattern=[[step, width]], channel_multiplier=1))

            const(nc.gpsimd.memset(ident[:], 0.0))
            picked(ident[:], 0, -1, ALU.not_equal, 1.0)
            const(nc.gpsimd.memset(ones[:], 1.0))
            const(nc.gpsimd.memset(eps[:], EPS))
            for i, width in enumerate((D, DI // NG, 2 * DH)):
                const(nc.gpsimd.memset(mean_col[:, i:i + 1], 1.0 / width))
            for h in range(NH):
                const(nc.gpsimd.memset(slopes[:, h:h + 1], 2.0 ** (-8.0 * (h + 1) / NH)))
            const(nc.gpsimd.memset(tri[:], 0.0))
            picked(tri[:], 0, -1, ALU.is_gt, 1.0)
            const(nc.gpsimd.memset(last_row[:], 0.0))
            picked(last_row[:], -(P - 1), 0, ALU.not_equal, 1.0)
            assert n == N_CONST, n

            split_lo(pool, MIX, 0, 0)
            split_lo(pool, MIX, 1, 1)
            boundary_pool(pool, 0)
            mix_pool(pool, 0, first=True)
            with pool.Fori(1, NG) as g:
                mix_pool(pool, g)
            ahead(split_lo, pool, MIX, MIX.units + 1)
            out_phase_pool(pool, SOUT, out_halves, 1)
            ffn_pool(pool, UP0)
            out_phase_pool(pool, DN0, out_halves, 2)
            pool.wait_ge(stat_ready, norm_no["pre2"] + 1)
            nc.gpsimd.iota(dist_i[:], [[1, S]], base=P - S, channel_multiplier=-1).then_inc(dist_made, 1)
            pool.wait_ge(dist_made, 1)
            nc.gpsimd.tensor_copy(dist[:], dist_i[:]).then_inc(dist_made, 1)
            pool.wait_ge(dist_made, 2)
            nc.gpsimd.affine_select(out=dist[:], in_=dist[:], compare_op=ALU.is_ge, fill=MASKED, base=S - P,
                                    pattern=[[-1, S]], channel_multiplier=1).then_inc(dist_made, 1)

            def att_pool(eng, h, b):
                for j in range(3):
                    if not (isinstance(h, int) and (h >= NH or (h == 0 and j == 0))):
                        ahead(split_lo, eng, QKV, 3 * h + 1 + j, 3 * b + 1 + j)
            att_rounds(pool, att_pool)
            ahead(split_lo, pool, QKV, QKV.units + 1)
            out_phase_pool(pool, AOUT, out_wholes, 3)
            ffn_pool(pool, UP1)
            out_phase_pool(pool, DN1, out_halves, 4)

        @block.scalar
        def _(act):
            act.wait_ge(par_in, 16)
            act.wait_ge(x_in_s, 16)
            act.wait_ge(consts, N_CONST)
            split_hi(act, MIX, 0, 0)
            split_hi(act, MIX, 1, 1)
            act.wait_ge(lam_dots, 1)
            nc.scalar.activation(lam_s[:, 2:4], lam_s[:, 0:2], ACT.Exp).then_inc(lam_exps, 1)
            boundary_act(act, 0)
            mix_act(act, 0, first=True, before=False)
            with act.Fori(1, NG) as g:
                mix_act(act, g)
            ahead(split_hi, act, MIX, MIX.units + 1)
            act.wait_ge(y_normed, 2 * NG - 2)
            act.wait_ge(seg_ready, NG)
            act.wait_ge(prev_ready, NG)
            act.wait_ge(cs_ready, NG)
            y_split_act(act, range(YC // 2))
            mix_act(act, NG, proj=False)
            for k in range(YC // 2, YC):
                if k >= YC - 2:
                    act.wait_ge(y_normed, k + 1)
                y_split_act(act, [k])
            out_phase_act(act, SOUT, out_halves, 1)
            ffn_act(act, UP0, 0)
            out_phase_act(act, DN0, out_halves, 2)
            att_rounds(act, att_act)
            ahead(split_hi, act, QKV, QKV.units + 1)
            out_phase_act(act, AOUT, out_wholes, 3)
            ffn_act(act, UP1, 1)
            out_phase_act(act, DN1, out_halves, 4)

        @block.vector
        def _(dve):
            dve.wait_ge(par_in, 16)
            dve.wait_ge(x_in_s, 16)
            dve.wait_ge(lam_in_s, 16)
            dve.wait_ge(consts, N_CONST)
            ch(nc.vector.tensor_tensor(lam_p[:], lam_v[:, 0:2 * DH], lam_v[:, 2 * DH:4 * DH], ALU.mult))
            dve.wait_ge(dve_done, ch.value())
            nc.vector.tensor_reduce(lam_s[:, 0:2], lam_p[:].rearrange("p (a d) -> p a d", a=2), AX.X,
                                    ALU.add).then_inc(lam_dots, 1)
            ch(nc.vector.tensor_scalar(gsub[:], par[:, SUBLN:SUBLN + 1], 1.0 - LAMBDA_INIT, None, ALU.mult))
            ch(nc.vector.memset(ug_s[:, 0:SSM_T - 1], 0.0))
            dve.wait_ge(lam_exps, 1)
            ch(nc.vector.tensor_tensor(lam_s[:, 4:5], lam_s[:, 3:4], lam_s[:, 2:3], ALU.subtract))
            dve.wait_ge(dve_done, ch.value())
            ch(nc.vector.tensor_scalar(lam_s[:, 4:5], lam_s[:, 4:5], -LAMBDA_INIT, None, ALU.add))
            dve.wait_ge(dve_done, ch.value())
            boundary_dve(dve, 0)
            dve.wait_ge(unit_done, 1)
            nc.vector.tensor_tensor(d_v[:], bank[0][0:HS, :], r_pre[0:HS, :], ALU.mult).then_inc(evac["in"], 1)
            dve.wait_ge(evac["in"], 1)
            mix_dve(dve, 0, first=True, before=False)
            with dve.Fori(1, NG) as g, ch.loop(g, 1, NG - 1, MIX_CHAIN):
                mix_dve(dve, g)
            y_split_dve(dve, range(YC // 2))
            mix_dve(dve, NG, proj=False)
            y_split_dve(dve, range(YC // 2, YC))
            boundary_dve(dve, 1)
            ffn_dve(dve, UP0, 0)
            boundary_dve(dve, 2)
            dve.wait_ge(dist_made, 3)
            att_rounds(dve, att_dve, chained=ATT_CHAIN)
            boundary_dve(dve, 3)
            ffn_dve(dve, UP1, 1)
            boundary_dve(dve, 4)

        @block.tensor
        def _(pe):
            pe.wait_ge(consts, N_CONST)
            boundary_pe(pe, 0, MIX)
            mix_pe(pe, 0, skip_x0=True, before=False)
            with pe.Fori(1, NG) as g:
                mix_pe(pe, g)

            def mid(q):
                if q == 0:
                    pe.wait_ge(ysq_ready, 2 * NG)
                    norm_stat([yt[:, 0, :], yt[:, 1, :]], 1)
                elif q == 1:
                    norm_bcast(pe, norm_no["group"] + NG - 1)

            mix_y_pe(pe, NG)
            out_halves_pe(pe, SOUT, 0, y_hi, y_lo, KC, ready=lambda k: pe.wait_ge(ylo_ready, k + 1), mid=mid)
            with pe.Fori(1, KC // 2) as i:
                out_halves_pe(pe, SOUT, i, y_hi, y_lo, KC)
            boundary_pe(pe, 1, UP0)
            ffn_pe(pe, UP0, DN0, 0)
            boundary_pe(pe, 2, QKV)
            att_rounds(pe, att_pe)
            for j in range(2):
                pe.wait_ge(lo_made, AOUT.U0 + j + 1)
                wait_bank(pe, AOUT, j)
            for c in range(KC):
                pe.wait_ge(olo_ready, c + 1)
                for j in range(2):
                    last = product(acc_of(AOUT, j), slot_of(AOUT, j), c, o_hi[:, c, :], o_lo[:, c, :],
                                   c == 0, c == KC - 1)
                    if c == KC - 1:
                        last.then_inc(unit_done, 1)
            with pe.Fori(1, KC // 2) as i:
                for s in range(2):
                    pe.wait_ge(lo_made, AOUT.U0 + 2 * i + s + 1)
                    wait_bank(pe, AOUT, 2 * i + s)
                    for c in range(KC):
                        last = product(acc_of(AOUT, s), slot_of(AOUT, s), c, o_hi[:, c, :], o_lo[:, c, :],
                                       c == 0, c == KC - 1)
                    last.then_inc(unit_done, 1)
            boundary_pe(pe, 3, UP1)
            ffn_pe(pe, UP1, DN1, 1)
            boundary_pe(pe, 4)


def _tiles(w, cols, k0=0, k1=None):
    part = w[k0:k1, cols:cols + P]
    return part.reshape(-1, P, P).transpose(1, 0, 2).reshape(P, -1)


def _halves(w):
    k = w.shape[0] // 2
    return np.stack([_tiles(w, (2 * i + s) * P, h * k, (h + 1) * k)
                     for i in range(KC // 2) for h in range(2) for s in range(2)])


def _by_chunk(v):
    return v.reshape(-1, P).T


def _pack(a):
    par = np.zeros((P, NPAR), np.float32)
    for layer in range(2):
        for kind, name in enumerate(("norm_mix_pre", "norm_mix_post", "norm_ffn_pre", "norm_ffn_post")):
            c = NORM0 + (layer * 4 + kind) * KC
            par[:, c:c + KC] = _by_chunk(a[name][layer])
    cw, cb, d, ng = a["ssm_conv_w"][0], a["ssm_conv_b"][0], a["ssm_D"][0], a["ssm_norm_g"][0]
    for g in range(NG):
        c = SSM0 + g * SSMW
        for f in (2 * g * P, (2 * g + 1) * P, DI + g * P, DI + NG * P + g * P):
            par[:, c:c + SSM_T] = cw[:, f:f + P].T
            par[:, c + SSM_T] = cb[f:f + P]
            c += SSM_T + 1
        for jj in range(2):
            par[0:HD, c + jj] = d[HG * g + 2 * jj]
            par[HD:P, c + jj] = d[HG * g + 2 * jj + 1]
        par[:, c + 2:c + 4] = _by_chunk(ng[2 * g * P:2 * (g + 1) * P])
    for layer in range(2):
        cw, cb = a["ffn_conv_w"][layer], a["ffn_conv_b"][layer]
        for m in range(FC):
            for s, f in enumerate((m * P, DFF + m * P)):
                c = FFN0 + (layer * FC + m) * FFNW + s * (FFN_T + 1)
                par[:, c:c + FFN_T] = cw[:, f:f + P].T
                par[:, c + FFN_T] = cb[f:f + P]
    par[:, SUBLN] = a["attn_subln_g"][0]
    par[0:HS, DTB] = a["ssm_dt_bias"][0]
    par[0:HS, ALOG] = a["ssm_A_log"][0]
    return par


def kernel(**inputs):
    from concourse import bacc
    from concourse.bass_utils import run_bass_kernel_spmd

    a = {k: np.asarray(v) for k, v in inputs.items()}
    w = a["ssm_w_in"][0]
    dt_cols = np.zeros((D, P), np.float32)
    dt_cols[:, 0:HS] = w[:, 2 * DI + 2 * NG * P:]
    mix = [_tiles(dt_cols, 0)]
    for g in range(NG):
        for c in (DI + 2 * g * P, DI + (2 * g + 1) * P, 2 * DI + g * P, 2 * DI + NG * P + g * P,
                  2 * g * P, (2 * g + 1) * P):
            mix.append(_tiles(w, c))
    qkv, wo = a["attn_w_qkv"][0], a["attn_w_out"][0]
    arrays = {
        "x_in": a["x"][0].T.reshape(KC, P, S).transpose(1, 0, 2),
        "w_mix": np.stack(mix),
        "w_sout": _halves(a["ssm_w_out"][0]),
        "w_up0": np.stack([_tiles(a["ffn_w_up"][0], s * DFF + m * P) for m in range(FC) for s in range(2)]),
        "w_dn0": _halves(a["ffn_w_down"][0]),
        "w_qkv": np.stack([_tiles(qkv, c * D + h * P) for h in range(NH) for c in range(3)]),
        "w_aout": np.stack([_tiles(wo, m * P) for m in range(KC)]),
        "w_up1": np.stack([_tiles(a["ffn_w_up"][1], s * DFF + m * P) for m in range(FC) for s in range(2)]),
        "w_dn1": _halves(a["ffn_w_down"][1]),
        "params": _pack(a),
        "lam_in": np.concatenate([a["attn_lambda_q1"][0], a["attn_lambda_q2"][0],
                                  a["attn_lambda_k1"][0], a["attn_lambda_k2"][0]]),
    }
    arrays = {k: np.ascontiguousarray(v) for k, v in arrays.items()}
    nc = bacc.Bacc("TRN2", target_bir_lowering=False, num_devices=1)
    args = [nc.dram_tensor(k, v.shape, F32, kind="ExternalInput").ap() for k, v in arrays.items()]
    out = nc.dram_tensor("out", (P, KC, S), F32, kind="ExternalOutput").ap()
    trunk(nc, *args, out)
    got = run_bass_kernel_spmd(nc, [arrays], core_ids=[0]).results[0]["out"]
    return np.ascontiguousarray(got.transpose(1, 0, 2).reshape(D, S).T).reshape(1, S, D)
```

```python
import math
from contextlib import ExitStack, contextmanager

import numpy as np

import concourse.bass as bass
from concourse import mybir

F32 = mybir.dt.float32
F32R = mybir.dt.float32r
ALU = mybir.AluOpType
ACT = mybir.ActivationFunctionType
AX = mybir.AxisListType

P = 128
S = 512
NB = S // P
D = 1024
KC = D // P
DI = 2 * D
YC = DI // P
NG, HG, HD = 8, 4, 64
HS = NG * HG
SSM_T, FFN_T = 4, 3
NH, DH = 8, 64
DFF = 2816
FC = DFF // P
HU = FC // 2
UW = HU * P
EPS = 1e-6
LAMBDA_INIT = 0.8 - 0.6 * math.exp(-0.3 * 1)
MASKED = -1e30

NORM0 = 0
SSM0 = NORM0 + 8 * KC
SSMW = 4 * (SSM_T + 1) + 4
FFN0 = SSM0 + NG * SSMW
FFNW = 2 * (FFN_T + 1)
SUBLN = FFN0 + 2 * FC * FFNW
DTB = SUBLN + 1
ALOG = DTB + 1
NPAR = ALOG + 1


class Phase:

    def __init__(self, units, chunks, width, kind, prev):
        self.units, self.chunks, self.width, self.kind, self.prev = units, chunks, width, kind, prev
        self.U0 = prev.U0 + prev.units if prev else 0
        self.Q0 = prev.Q0 + prev.chunks if prev else 0
        self.before = {"in": 0, "out": 0}
        if prev:
            self.before = dict(prev.before)
            self.before[prev.kind] += prev.chunks


def phases():
    made, prev = [], None
    for units, chunks, width, kind in (
            (1 + 6 * NG, 1 + 6 * NG, KC * P, "in"), (2 * KC, KC, KC * P, "out"),
            (2 * FC, 2 * FC, KC * P, "in"), (2 * KC, KC, UW, "out"),
            (3 * NH, 3 * NH, KC * P, "in"), (KC, KC, KC * P, "out"),
            (2 * FC, 2 * FC, KC * P, "in"), (2 * KC, KC, UW, "out")):
        prev = Phase(units, chunks, width, kind, prev)
        made.append(prev)
    return made


class Chain:

    def __init__(self, sem):
        self.sem, self.n, self.dyn = sem, 0, 0

    def __call__(self, ins):
        ins.then_inc(self.sem, 1)
        self.n += 1

    def value(self):
        return self.n + self.dyn

    @contextmanager
    def loop(self, i, start, trips, per):
        first = self.n
        self.dyn = (i - start) * per
        yield
        assert self.n - first == per, (self.n - first, per)
        self.dyn = 0
        self.n = first + per * trips


def trunk(nc, x_in, w_mix, w_sout, w_up0, w_dn0, w_qkv, w_aout, w_up1, w_dn1, params, lam_in, out):
    ctx = ExitStack()
    with ctx:
        MIX, SOUT, UP0, DN0, QKV, AOUT, UP1, DN1 = PH = phases()
        dram_of = dict(zip(PH, (w_mix, w_sout, w_up0, w_dn0, w_qkv, w_aout, w_up1, w_dn1)))

        def sb(name, shape, dt=F32, scope=ctx):
            return scope.enter_context(nc.sbuf_tensor(name, shape, dt))

        def sem(name):
            return ctx.enter_context(nc.semaphore(name))

        x = sb("x", [P, KC, S])
        raw = sb("raw", [P, 2, UW])
        w_hi = sb("w_hi", [P, 2, UW], F32R)
        w_lo = sb("w_lo", [P, 2, UW], F32R)
        par = sb("par", [P, NPAR])
        lam_v = sb("lam_v", [P, 4 * DH])
        lam_p = sb("lam_p", [P, 2 * DH])
        lam_s = sb("lam_s", [P, 8])
        gsub = sb("gsub", [P, 1])
        slopes = sb("slopes", [P, NH])
        eps = sb("eps", [P, 1])
        ident = sb("ident", [P, P])
        ones = sb("ones", [P, P])
        mean_col = sb("mean_col", [P, 3])
        root = sb("root", [P, NB])
        spare = sb("spare", [P, 1])
        rcol = sb("rcol", [P, NB])
        diag = sb("diag", [P, NB, P])
        rcol_hi, rcol_lo = sb("rcol_hi", [P, NB], F32R), sb("rcol_lo", [P, NB], F32R)
        diag_hi, diag_lo = sb("diag_hi", [P, NB, P], F32R), sb("diag_lo", [P, NB, P], F32R)
        ones_r = sb("ones_r", [P, P], F32R)
        r_pre = sb("r_pre", [P, S])
        ssq = sb("ssq", [P, S])
        sq = sb("sq", [P, 2, S])
        hn_lo = sb("hn_lo", [P, KC, S], F32R)
        with ExitStack() as lap:
            mbuf = sb("mbuf", [P, KC, S], scope=lap)
        hn_hi = sb("hn_hi", [P, KC, S], F32R)

        with ExitStack() as ssm:
            with ExitStack() as lap:
                ybuf = sb("ybuf", [P, YC, S], scope=lap)
            y_lo = sb("y_lo", [P, YC, S], F32R, scope=ssm)
            with ExitStack() as lap:
                acs_bc = sb("acs_bc", [P, HG, S], scope=lap)
                ecs_bc = sb("ecs_bc", [P, HG, S], scope=lap)
                xc = sb("xc", [P, 2, S], scope=lap)
                bT = sb("bT", [P, S], scope=lap)
                cT = sb("cT", [P, S], scope=lap)
                ug_s = sb("ug_s", [P, SSM_T - 1 + S], scope=lap)
                cv_s = sb("cv_s", [P, S], scope=lap)
                btok = sb("btok", [P, NB, P], scope=lap)
                xdd = sb("xdd", [P, NB, HG, HD], scope=lap)
            y_hi = sb("y_hi", [P, YC, S], F32R, scope=ssm)
            sb("gap", [P, 1024], scope=ssm)
            with ExitStack() as lap:
                d_v = sb("d_v", [HS, S], scope=lap)
                d_e = sb("d_e", [HS, S], scope=lap)
                d_z = sb("d_z", [HS, S], scope=lap)
                t_v, t_w, t_e, t_z, t_p = (sb(n, [P, NB * HS], scope=lap)
                                           for n in ("t_v", "t_w", "t_e", "t_z", "t_p"))
                d_acs = sb("d_acs", [HS, S], scope=lap)
                d_ea = sb("d_ea", [HS, 1], scope=lap)
                last_row = sb("last_row", [P, P], scope=lap)
            xdt = sb("xdt", [P, NB, HG, HD], scope=ssm)
            m_t = sb("m_t", [P, HG, S], scope=ssm)
            cs_t = sb("cs_t", [P, HG, S - P], scope=ssm)
            cbm = sb("cbm", [P, S], scope=ssm)
            prev = sb("prev", [P, NB - 1, HG, HD], scope=ssm)
            pdec = sb("pdec", [P, HG, HD], scope=ssm)
            yt = sb("yt", [P, 2, S], scope=ssm)
            zs = sb("zs", [P, 2, S], scope=ssm)
            tri = sb("tri", [P, P], scope=ssm)
            dt_tok = sb("dt_tok", [P, NB, HS], scope=ssm)
            nacs = sb("nacs", [P, NB, HS], scope=ssm)
            acs_tok = sb("acs_tok", [P, NB, HS], scope=ssm)
            wdec = sb("wdec", [P, NB, HS], scope=ssm)
            nac_g = sb("nac_g", [P, NB, HG], scope=ssm)
        with ExitStack() as ffn:
            h_hi = sb("h_hi", [P, FC, S], F32R, scope=ffn)
            h_lo = sb("h_lo", [P, FC, S], F32R, scope=ffn)
            ug_f = sb("ug_f", [P, FFN_T - 1 + S], scope=ffn)
            cg = sb("cg", [P, S], scope=ffn)
            cu = sb("cu", [P, S], scope=ffn)
            sg = sb("sg", [P, S], scope=ffn)
            hb = sb("hb", [P, S], scope=ffn)
        with ExitStack() as att:
            o_hi = sb("o_hi", [P, NH, S], F32R, scope=att)
            o_lo = sb("o_lo", [P, NH, S], F32R, scope=att)
            qT = sb("qT", [P, 2, S], scope=att)
            kT = sb("kT", [P, 2, S], scope=att)
            vT = sb("vT", [P, 2, S], scope=att)
            vtok = sb("vtok", [P, 2, NB, P], scope=att)
            dist_i = sb("dist_i", [P, S], mybir.dt.int32, scope=att)
            dist = sb("dist", [P, S], scope=att)
            sc = sb("sc", [P, 2, 2, S], scope=att)
            pr = sb("pr", [P, 2, 2, S], scope=att)
            at = sb("at", [P, NB, S], scope=att)
            aT = sb("aT", [P, NB, S], scope=att)
            ob = sb("ob", [P, S], scope=att)
            osq = sb("osq", [P, S], scope=att)
            on = sb("on", [P, S], scope=att)
            nmx = sb("nmx", [P, 2, 2], scope=att)
            den = sb("den", [P, 2, 2], scope=att)
            cf = sb("cf", [P, 2, 2], scope=att)

        bank = [ctx.enter_context(nc.psum_tensor(f"bank{i}", [P, S], F32)) for i in range(2)]
        b_norm = ctx.enter_context(nc.psum_tensor("b_norm", [P, S], F32))
        b_x = ctx.enter_context(nc.psum_tensor("b_x", [P, 2, S], F32))
        b_cb = ctx.enter_context(nc.psum_tensor("b_cb", [P, S], F32))
        b_y = ctx.enter_context(nc.psum_tensor("b_y", [P, 2, S], F32))
        scores_in = (b_x, b_y)
        b_tr, b_pv = b_cb, b_norm

        scratch = nc.dram_tensor("scratch", [2, HS, S], F32).ap()

        par_in, lam_in_s, x_in_s = sem("par_in"), sem("lam_in_s"), [sem(f"x_in{m}") for m in range(KC)]
        raw_in = [sem("raw_in0"), sem("raw_in1")]
        acs_out, ecs_out, acs_in, ecs_in = sem("acs_out"), sem("ecs_out"), sem("acs_in"), sem("ecs_in")
        y_sent = sem("y_sent")
        hi_made, lo_made, unit_done = sem("hi_made"), sem("lo_made"), sem("unit_done")
        evac = {"in": sem("evac_in"), "out": sem("evac_out")}
        dve_done = sem("dve_done")
        consts = sem("consts")
        sq_ready, sq_added = sem("sq_ready"), sem("sq_added")
        stat_ready, root_ready, diag_ready, bc_ready = (
            sem("stat_ready"), sem("root_ready"), sem("diag_ready"), sem("bc_ready"))
        rpre_copied = sem("rpre_copied")
        scaled, x_new, x_new_pool = sem("scaled"), sem("x_new"), sem("x_new_pool")
        hnhi_ready, hnlo_ready = sem("hnhi_ready"), sem("hnlo_ready")
        conv_ready = sem("conv_ready")
        dtv_ready, dtv_back, dt_ready, dt_back = (
            sem("dtv_ready"), sem("dtv_back"), sem("dt_ready"), sem("dt_back"))
        dt_in, dt_exp, al_exp, acs_ready, ecs_ready = (
            sem("dt_in"), sem("dt_exp"), sem("al_exp"), sem("acs_ready"), sem("ecs_ready"))
        dtr_ready, tok_ready, tot_ready, dec_in, dec_exp = (
            sem("dtr_ready"), sem("tok_ready"), sem("tot_ready"), sem("dec_in"), sem("dec_exp"))
        silu_ready = sem("silu_ready")
        trb_ready, trx_ready, cb_ready, st_ready, y_ready = (
            sem("trb_ready"), sem("trx_ready"), sem("cb_ready"), sem("st_ready"), sem("y_ready"))
        btok_ready, skip_ready, seg_ready, seg_exp = (
            sem("btok_ready"), sem("skip_ready"), sem("seg_ready"), sem("seg_exp"))
        xw_ready, cbm_ready, prev_ready, m_ready, cs_ready = (
            sem("xw_ready"), sem("cbm_ready"), sem("prev_ready"), sem("m_ready"), sem("cs_ready"))
        y_gated, ysq_ready, ysq_added, y_normed = (
            sem("y_gated"), sem("ysq_ready"), sem("ysq_added"), sem("y_normed"))
        yhi_ready, ylo_ready = sem("yhi_ready"), sem("ylo_ready")
        table_in = sem("table_in")
        gate_ready, hb_ready, hhi_ready, hlo_ready = (
            sem("gate_ready"), sem("hb_ready"), sem("hhi_ready"), sem("hlo_ready"))
        s_ready, s_taken, mx_ready, p_ready, a_ready, tr_ready, tr_copied = (
            sem("s_ready"), sem("s_taken"), sem("mx_ready"), sem("p_ready"),
            sem("a_ready"), sem("tr_ready"), sem("tr_copied"))
        pv_ready, ob_ready, on_ready, ohi_ready, olo_ready = (
            sem("pv_ready"), sem("ob_ready"), sem("on_ready"), sem("ohi_ready"), sem("olo_ready"))
        lam_dots, lam_exps, dist_made = sem("lam_dots"), sem("lam_exps"), sem("dist_made")

        ch = Chain(dve_done)
        N_CONST = 19
        MIX_CHAIN = 4 * (SSM_T - 1) + 11
        ATT_CHAIN = 2 * (4 * 3 + 4)

        order = ["pre0", "group"] + ["post1", "pre1", "post2", "pre2", "head"] + ["post3", "pre3", "post4"]
        norm_no, n = {}, 0
        for name in order:
            norm_no[name] = n
            n += {"group": NG, "head": NH}.get(name, 1)
        sum_no = {name: n for n, name in enumerate(x for x in order if x not in ("group", "head"))}

        def gain(layer, kind, m):
            c = NORM0 + (layer * 4 + kind) * KC + m
            return par[:, c:c + 1]

        def col(c):
            return par[:, bass.ds(c, 1)]

        def slot_of(ph, j):
            return (ph.U0 + j) % 2

        def acc_of(ph, j):
            return bank[(ph.Q0 + j) % 2]

        def load_unit(sp, ph, j, rep):
            slot = slot_of(ph, rep)
            if not (isinstance(j, int) and ph.U0 + j < 2):
                sp.wait_ge(lo_made, ph.U0 + j - 1)
            sp.dma_start(raw[:, slot, 0:ph.width], dram_of[ph][j]).then_inc(raw_in[slot], 16)

        def split_hi(act, ph, j, rep):
            slot, U = slot_of(ph, rep), ph.U0 + j
            act.wait_ge(raw_in[slot], 8 * U + (16 - 8 * slot))
            if not (isinstance(j, int) and U < 2):
                act.wait_ge(unit_done, U - 1)
            nc.scalar.activation(w_hi[:, slot, 0:ph.width], raw[:, slot, 0:ph.width],
                                 ACT.Copy).then_inc(hi_made, 1)

        def split_lo(pool, ph, j, rep):
            slot = slot_of(ph, rep)
            pool.wait_ge(hi_made, ph.U0 + j + 1)
            nc.gpsimd.tensor_tensor(w_lo[:, slot, 0:ph.width], raw[:, slot, 0:ph.width],
                                    w_hi[:, slot, 0:ph.width].bitcast(F32), ALU.subtract).then_inc(lo_made, 1)

        def split_lo_dve(dve, ph, j):
            slot = slot_of(ph, j)
            dve.wait_ge(hi_made, ph.U0 + j + 1)
            nc.vector.tensor_tensor(w_lo[:, slot, 0:ph.width], raw[:, slot, 0:ph.width],
                                    w_hi[:, slot, 0:ph.width].bitcast(F32), ALU.subtract).then_inc(lo_made, 1)

        def ahead(split, eng, ph, j, rep=None):
            if isinstance(j, int) and j >= ph.units:
                k = PH.index(ph) + 1
                if k < len(PH):
                    split(eng, PH[k], j - ph.units, j - ph.units)
            else:
                split(eng, ph, j, j if rep is None else rep)

        def wait_bank(pe, ph, j):
            if isinstance(j, int) and j < 2:
                if ph.prev is not None:
                    pv = ph.prev
                    pe.wait_ge(evac[pv.kind], pv.before[pv.kind] + pv.chunks - 1 + j)
            else:
                pe.wait_ge(evac[ph.kind], ph.before[ph.kind] + j - 1)

        def product(acc, slot, c, hi, lo, first, last):
            wh, wl = w_hi[:, slot, c * P:(c + 1) * P], w_lo[:, slot, c * P:(c + 1) * P]
            nc.tensor.matmul(acc[:], wh, hi, start=first, stop=False)
            nc.tensor.matmul(acc[:], wh, lo, start=False, stop=False)
            return nc.tensor.matmul(acc[:], wl, hi, start=False, stop=last)

        def in_unit(pe, ph, j, rep):
            pe.wait_ge(lo_made, ph.U0 + j + 1)
            wait_bank(pe, ph, j)
            for c in range(KC):
                last = product(acc_of(ph, rep), slot_of(ph, rep), c, hn_hi[:, c, :], hn_lo[:, c, :],
                               c == 0, c == KC - 1)
            last.then_inc(unit_done, 1)

        def norm_stat(squares, mean):
            for b in range(NB):
                last = nc.tensor.matmul(b_norm[:, b:b + 1], squares[:, b * P:(b + 1) * P],
                                        mean_col[:, mean:mean + 1], start=True, stop=True)
            last.then_inc(stat_ready, 1)

        def norm_root(act, n):
            act.wait_ge(stat_ready, n + 1)
            nc.scalar.activation(root[:], b_norm[:, 0:NB], ACT.Sqrt, bias=eps[:]).then_inc(root_ready, 1)

        def norm_diag(dve, n, split=False):
            def on_diagonal(dst, r):
                return nc.vector.tensor_tensor(dst[:], ident[:].unsqueeze(1).to_broadcast([P, NB, P]),
                                               r.unsqueeze(2).to_broadcast([P, NB, P]), ALU.mult)

            dve.wait_ge(root_ready, n + 1)
            if not (isinstance(n, int) and n < 1):
                dve.wait_ge(diag_ready, n)
                dve.wait_ge(bc_ready, n)
            ch(nc.vector.reciprocal(rcol[:], root[:]))
            dve.wait_ge(dve_done, ch.value())
            if split:
                ch(nc.vector.tensor_copy(rcol_hi[:], rcol[:]))
                dve.wait_ge(dve_done, ch.value())
                ch(nc.vector.tensor_tensor(rcol_lo[:], rcol[:], rcol_hi[:].bitcast(F32), ALU.subtract))
                ch(on_diagonal(diag_hi, rcol_hi[:].bitcast(F32)))
                dve.wait_ge(dve_done, ch.value())
                on_diagonal(diag_lo, rcol_lo[:].bitcast(F32)).then_inc(diag_ready, 1)
            else:
                on_diagonal(diag, rcol[:]).then_inc(diag_ready, 1)

        def norm_bcast(pe, n, split=False):
            pe.wait_ge(diag_ready, n + 1)
            if split:
                nc.tensor.matmul(b_norm[:], ones_r[:], diag_hi[:].rearrange("p b t -> p (b t)"),
                                 start=True, stop=False)
                nc.tensor.matmul(b_norm[:], ones_r[:], diag_lo[:].rearrange("p b t -> p (b t)"),
                                 start=False, stop=True).then_inc(bc_ready, 1)
            else:
                nc.tensor.matmul(b_norm[:], ones[:], diag[:].rearrange("p b t -> p (b t)"),
                                 start=True, stop=True).then_inc(bc_ready, 1)

        def norm_before(n):
            return norm_no[[k for k in sum_no if sum_no[k] == n - 1][0]]

        def square(act, n, m, rep, src):
            if isinstance(m, int) and m < 2:
                if n and m == 0:
                    act.wait_ge(sq_added, (KC - 1) * n)
                elif n:
                    act.wait_ge(stat_ready, norm_before(n) + 1)
            else:
                act.wait_ge(sq_added, (KC - 1) * n + m - 1)
            return nc.scalar.activation(sq[:, rep % 2, :], src, ACT.Square)

        def add_square(pool, name, m, rep):
            n = sum_no[name]
            if isinstance(m, int) and m == KC - 1:
                return
            if isinstance(m, int) and m == 0:
                if n:
                    pool.wait_ge(stat_ready, norm_before(n) + 1)
            else:
                pool.wait_ge(sq_added, (KC - 1) * n + m)
            pool.wait_ge(sq_ready, KC * n + m + 1)
            if isinstance(m, int) and m == 0:
                nc.gpsimd.tensor_copy(ssq[:], sq[:, 0, :]).then_inc(sq_added, 1)
            else:
                nc.gpsimd.tensor_tensor(ssq[:], ssq[:], sq[:, rep % 2, :], ALU.add).then_inc(sq_added, 1)

        def sum_stat(pe, name):
            n = sum_no[name]
            pe.wait_ge(sq_added, (KC - 1) * (n + 1))
            for b in range(NB):
                nc.tensor.matmul(b_norm[:, b:b + 1], ssq[:, b * P:(b + 1) * P], mean_col[:, 0:1],
                                 start=b == 0, stop=False)
            pe.wait_ge(sq_ready, KC * (n + 1))
            for b in range(NB):
                last = nc.tensor.matmul(b_norm[:, b:b + 1], sq[:, (KC - 1) % 2, b * P:(b + 1) * P],
                                        mean_col[:, 0:1], start=False, stop=b == NB - 1)
            last.then_inc(stat_ready, 1)

        GAINS = {0: (None, (0, 0)), 1: ((0, 1), (0, 2)), 2: ((0, 3), (1, 0)), 3: ((1, 1), (1, 2)), 4: ((1, 3), None)}

        POOL_ADDS = {b: (1, 3, 5) for b in range(1, 4)}
        POOL_ADDS[4] = (1, 3, 5, 6)

        def wait_x(eng, b, m):
            by_pool = m in POOL_ADDS[b]
            n = sum(len(POOL_ADDS[k]) if by_pool else KC - len(POOL_ADDS[k]) for k in range(1, b))
            n += sum((k in POOL_ADDS[b]) == by_pool for k in range(m + 1))
            eng.wait_ge(x_new_pool if by_pool else x_new, n)

        def boundary_pe(pe, b, nxt=None):
            if b:
                pe.wait_ge(rpre_copied, b)
                sum_stat(pe, f"post{b}")
                norm_bcast(pe, norm_no[f"post{b}"])
            if nxt is None:
                return
            for j in range(2):
                pe.wait_ge(lo_made, nxt.U0 + j + 1)
                wait_bank(pe, nxt, j)
            for c in range(KC):
                if c == KC - 1:
                    if b:
                        wait_x(pe, b, KC - 1)
                    sum_stat(pe, f"pre{b}")
                pe.wait_ge(hnlo_ready, KC * b + c + 1)
                for j in range(2):
                    last = product(acc_of(nxt, j), slot_of(nxt, j), c, hn_hi[:, c, :], hn_lo[:, c, :],
                                   c == 0, c == KC - 1)
                    if c == KC - 1:
                        last.then_inc(unit_done, 1)
            norm_bcast(pe, norm_no[f"pre{b}"])

        def boundary_act(act, b, nxt=None):
            if b:
                norm_root(act, norm_no[f"post{b}"])
            if GAINS[b][1] is None:
                return
            for m in range(KC):
                if b:
                    wait_x(act, b, m)
                else:
                    act.wait_ge(x_in_s[m], 16)
                nc.scalar.activation(hn_hi[:, m, :], x[:, m, :], ACT.Copy,
                                     scale=gain(*GAINS[b][1], m)).then_inc(hnhi_ready, 1)
                square(act, sum_no[f"pre{b}"], m, m, x[:, m, :]).then_inc(sq_ready, 1)
            norm_root(act, norm_no[f"pre{b}"])
            ahead(split_hi, act, nxt, 2)
            act.wait_ge(bc_ready, norm_no[f"pre{b}"] + 1)
            nc.scalar.activation(r_pre[:], b_norm[:], ACT.Copy).then_inc(rpre_copied, 1)

        def boundary_pool(pool, b, nxt=None):
            def add(m):
                pool.wait_ge(scaled, sum(len(POOL_ADDS[k]) for k in range(1, b)) + POOL_ADDS[b].index(m) + 1)
                nc.gpsimd.tensor_tensor(x[:, m, :], x[:, m, :], mbuf[:, m, :], ALU.add).then_inc(x_new_pool, 1)

            for m in range(KC):
                if b and m in POOL_ADDS[b]:
                    add(m)
                if nxt is not None and m:
                    add_square(pool, f"pre{b}", m - 1, m - 1)
            if nxt is not None:
                pool.wait_ge(lo_made, nxt.U0 + 3)

        def boundary_dve(dve, b, nxt=None):
            def lo(m):
                dve.wait_ge(hnhi_ready, KC * b + m + 1)
                nc.vector.scalar_tensor_tensor(hn_lo[:, m, :], x[:, m, :], gain(*GAINS[b][1], m),
                                               hn_hi[:, m, :].bitcast(F32), ALU.mult, ALU.subtract
                                               ).then_inc(hnlo_ready, 1)

            if b:
                norm_diag(dve, norm_no[f"post{b}"])
                dve.wait_ge(bc_ready, norm_no[f"post{b}"] + 1)
            def scale(m):
                ins = nc.vector.scalar_tensor_tensor(mbuf[:, m, :], mbuf[:, m, :], gain(*GAINS[b][0], m),
                                                     b_norm[:], ALU.mult, ALU.mult)
                if m in POOL_ADDS[b]:
                    ins.then_inc(scaled, 1)
                else:
                    ch(ins)
                    made[m] = ch.value()

            made = {}
            if b:
                scale(0)
            for m in range(KC):
                if b and m and m + 1 < KC:
                    scale(m + 1)
                if b and m not in POOL_ADDS[b]:
                    dve.wait_ge(dve_done, made[m])
                    nc.vector.tensor_tensor(x[:, m, :], x[:, m, :], mbuf[:, m, :], ALU.add).then_inc(x_new, 1)
                if b and m == 0:
                    scale(1)
                if m and GAINS[b][1] is not None:
                    lo(m - 1)
            if GAINS[b][1] is not None:
                lo(KC - 1)
                norm_diag(dve, norm_no[f"pre{b}"])
                split_lo_dve(dve, nxt, 2)
                dve.wait_ge(rpre_copied, b + 1)

        def out_halves_pe(pe, ph, i, hi, lo, tiles, ready=None, mid=None):
            for q in range(4):
                half, s = divmod(q, 2)
                pe.wait_ge(lo_made, ph.U0 + 4 * i + q + 1)
                if half == 0:
                    wait_bank(pe, ph, 2 * i + s)
                for c in range(tiles):
                    k = half * tiles + c
                    if ready is not None and s == 0:
                        ready(k)
                    last = product(acc_of(ph, s), slot_of(ph, q), c, hi[:, k, :], lo[:, k, :],
                                   k == 0, k == 2 * tiles - 1)
                last.then_inc(unit_done, 1)
                if mid is not None:
                    mid(q)

        def out_chunk_act(act, ph, m, rep, b, units_before):
            act.wait_ge(unit_done, ph.U0 + units_before)
            acc = acc_of(ph, rep)
            square(act, sum_no[f"post{b}"], m, rep, acc[:]).then_inc(sq_ready, 1)
            nc.scalar.activation(mbuf[:, m, :], acc[:], ACT.Copy).then_inc(evac["out"], 1)

        def out_halves(eng, ph, i, split, chunk, last=False):
            ahead(split, eng, ph, 4 * i + 2, 2)
            ahead(split, eng, ph, 4 * i + 3, 3)
            ahead(split, eng, ph, 4 * i + 4, 4)
            chunk(2 * i, 0, 4 * i + 3)
            if last:
                chunk(2 * i + 1, 1, 4 * i + 4)
            ahead(split, eng, ph, 4 * i + 5, 5)
            if not last:
                chunk(2 * i + 1, 1, 4 * i + 4)

        def out_wholes(eng, ph, i, split, chunk, last=False):
            ahead(split, eng, ph, 2 * i + 2, 2)
            chunk(2 * i, 0, 2 * i + 1)
            if last:
                chunk(2 * i + 1, 1, 2 * i + 2)
            ahead(split, eng, ph, 2 * i + 3, 3)
            if not last:
                chunk(2 * i + 1, 1, 2 * i + 2)

        def out_phase(eng, ph, body, split, chunk):
            n = KC // 2
            body(eng, ph, 0, split, chunk)
            with eng.Fori(1, n - 1) as i:
                body(eng, ph, i, split, chunk)
            body(eng, ph, n - 1, split, chunk, True)

        def out_phase_act(act, ph, body, b, nxt=None):
            def split(eng, ph, j, rep):
                if not (ph is SOUT and isinstance(j, int) and j in (2, 3)):
                    split_hi(eng, ph, j, rep)

            nc.scalar.activation(spare[:], eps[:], ACT.Sqrt).then_inc(table_in, 1)
            act.wait_ge(table_in, b)
            out_phase(act, ph, body, split, lambda m, rep, u: out_chunk_act(act, ph, m, rep, b, u))
            boundary_act(act, b, nxt)

        def out_phase_pool(pool, ph, body, b, nxt=None):
            out_phase(pool, ph, body, split_lo, lambda m, rep, u: add_square(pool, f"post{b}", m, rep))
            boundary_pool(pool, b, nxt)

        def conv(dve, ph, j, rep, ug, taps, wcol, dst, n_conv):
            dve.wait_ge(unit_done, ph.U0 + j + 1)
            if not (isinstance(n_conv, int) and n_conv == 0):
                dve.wait_ge(conv_ready, n_conv)
            nc.vector.tensor_tensor(ug[:, taps - 1:taps - 1 + S], acc_of(ph, rep)[:], r_pre[:],
                                    ALU.mult).then_inc(evac["in"], 1)
            dve.wait_ge(evac["in"], ph.before["in"] + j + 1)
            ch(nc.vector.tensor_scalar(dst, ug[:, taps - 1:taps - 1 + S], col(wcol + taps - 1), col(wcol + taps),
                                       ALU.mult, ALU.add))
            for t in range(taps - 1):
                dve.wait_ge(dve_done, ch.value())
                ins = nc.vector.scalar_tensor_tensor(dst, ug[:, t:t + S], col(wcol + t), dst, ALU.mult, ALU.add)
                if t < taps - 2:
                    ch(ins)
            ins.then_inc(conv_ready, 1)

        def mix_y_pe(pe, g):
            pe.wait_ge(m_ready, g)
            pe.wait_ge(cs_ready, g)
            pe.wait_ge(prev_ready, g)
            for jj in range(2):
                for c in range(NB):
                    for half in range(2):
                        hh = 2 * jj + half
                        dst = b_y[HD * half:HD * half + HD, jj, c * P:(c + 1) * P]
                        last = nc.tensor.matmul(dst, xdt[:, c, hh, :], m_t[:, hh, c * P:(c + 1) * P],
                                                start=True, stop=c == 0)
                        if c:
                            last = nc.tensor.matmul(dst, prev[:, c - 1, hh, :],
                                                    cs_t[:, hh, (c - 1) * P:c * P], start=False, stop=True)
            last.then_inc(y_ready, 1)

        def mix_pe(pe, g, skip_x0=False, before=True):
            if not skip_x0:
                in_unit(pe, MIX, 1 + 6 * g, 1)
            else:
                pe.wait_ge(dtv_ready, 1)
                for c in range(NB):
                    last = nc.tensor.transpose(b_cb[:, c * HS:(c + 1) * HS], d_v[:, c * P:(c + 1) * P],
                                               ident[0:HS, 0:HS])
                last.then_inc(dtv_back, 1)
            if before:
                mix_y_pe(pe, g)
            in_unit(pe, MIX, 2 + 6 * g, 2)
            in_unit(pe, MIX, 3 + 6 * g, 3)
            if before:
                pe.wait_ge(ysq_added, g)
                pe.wait_ge(btok_ready, g)
                norm_stat(yt[:, 0, :], 1)
            if skip_x0:
                pe.wait_ge(dt_ready, 1)
                for c in range(NB):
                    last = nc.tensor.transpose(b_cb[0:HS, c * P:(c + 1) * P], dt_tok[:, c, :], ident[:])
                last.then_inc(dt_back, 1)
            in_unit(pe, MIX, 4 + 6 * g, 4)
            if skip_x0:
                pe.wait_ge(acs_ready, 1)
                for c in range(NB):
                    last = nc.tensor.transpose(b_cb[:, c * HS:(c + 1) * HS], d_acs[:, c * P:(c + 1) * P],
                                               ident[0:HS, 0:HS])
                last.then_inc(dtr_ready, 1)
            in_unit(pe, MIX, 5 + 6 * g, 5)
            if skip_x0:
                pe.wait_ge(tok_ready, 1)
                nc.tensor.matmul(b_cb[:, 0:NB * HS], last_row[:], acs_tok[:].rearrange("p c h -> p (c h)"),
                                 start=True, stop=True).then_inc(tot_ready, 1)
            if before:
                norm_bcast(pe, norm_no["group"] + g - 1, split=True)
            pe.wait_ge(silu_ready, 6 * g + 4)
            if before:
                pe.wait_ge(prev_ready, g)
            for c in range(NB):
                for jj in range(2):
                    at_c = (c % 2) * 2 * P + jj * P
                    last = nc.tensor.transpose(b_x[:, c // 2, at_c:at_c + P], xc[:, jj, c * P:(c + 1) * P], ident[:])
            last.then_inc(trx_ready, 1)
            if before:
                pe.wait_ge(cbm_ready, g)
            else:
                pe.wait_ge(dec_in, 1)
            for c in range(NB):
                last = nc.tensor.matmul(b_cb[:, c * P:(c + 1) * P], bT[:, c * P:(c + 1) * P],
                                        cT[:, c * P:(c + 1) * P], start=True, stop=True)
            last.then_inc(cb_ready, 1)
            if before:
                pe.wait_ge(y_normed, 2 * g)
            else:
                pe.wait_ge(rpre_copied, 1)
            for c in range(NB):
                last = nc.tensor.transpose(b_norm[:, c * P:(c + 1) * P], bT[:, c * P:(c + 1) * P], ident[:])
            last.then_inc(trb_ready, 1)
            in_unit(pe, MIX, 6 + 6 * g, 6)
            pe.wait_ge(xw_ready, g + 1)
            pe.wait_ge(btok_ready, g + 1)
            for c in range(NB - 1):
                last = nc.tensor.matmul(b_x[:, c // 2, (c % 2) * 2 * P:(c % 2) * 2 * P + 2 * P], btok[:, c, :],
                                        xdd[:, c, :, :].rearrange("p h d -> p (h d)"), start=True, stop=True)
            last.then_inc(st_ready, 1)

        def mix_act(act, g, first=False, proj=True, before=True, mid=None):
            def silu(dst, src):
                nc.scalar.activation(dst, src, ACT.Silu).then_inc(silu_ready, 1)

            if proj:
                ahead(split_hi, act, MIX, 3 + 6 * g, 3)
                act.wait_ge(conv_ready, 4 * g + 1)
                if before:
                    act.wait_ge(trx_ready, g)
                silu(xc[:, 0, :], cv_s[:])
                if first:
                    act.wait_ge(dt_in, 1)
                    nc.scalar.activation(t_e[:], t_w[:], ACT.Exp).then_inc(dt_exp, 1)
                    nc.scalar.activation(d_ea[:], par[0:HS, ALOG:ALOG + 1], ACT.Exp).then_inc(al_exp, 1)
                ahead(split_hi, act, MIX, 4 + 6 * g, 4)
            if before:
                for jj in range(2):
                    act.wait_ge(y_gated, 2 * g - 1 + jj)
                    nc.scalar.activation(yt[:, jj, :], y_at(2 * g - 2 + jj), ACT.Square).then_inc(ysq_ready, 1)
            if proj:
                act.wait_ge(conv_ready, 4 * g + 2)
                silu(xc[:, 1, :], cv_s[:])
                if first:
                    act.wait_ge(acs_ready, 1)
                    nc.scalar.activation(d_z[:], d_acs[:], ACT.Exp).then_inc(ecs_ready, 1)
            if proj:
                ahead(split_hi, act, MIX, 5 + 6 * g, 5)
            if mid is not None:
                mid(0)
            if before:
                norm_root(act, norm_no["group"] + g - 1)
            if mid is not None:
                mid(1)
            if not proj:
                return
            act.wait_ge(conv_ready, 4 * g + 3)
            if before:
                act.wait_ge(cb_ready, g)
            silu(bT[:], cv_s[:])
            ahead(split_hi, act, MIX, 6 + 6 * g, 6)
            act.wait_ge(conv_ready, 4 * g + 4)
            if before:
                act.wait_ge(cs_ready, g)
            silu(cT[:], cv_s[:])
            act.wait_ge(silu_ready, 6 * g + 2)
            for jj in range(2):
                nc.scalar.activation(yt[:, jj, :], xc[:, jj, :], ACT.Copy,
                                     scale=col(SSM0 + SSMW * g + 4 * (SSM_T + 1) + jj)).then_inc(skip_ready, 1)
            ahead(split_hi, act, MIX, 7 + 6 * g, 7)
            act.wait_ge(evac["in"], 6 * g + 6)
            silu(zs[:, 0, :], zs[:, 0, :])
            if first:
                act.wait_ge(dec_in, 1)
                nc.scalar.activation(wdec[:], wdec[:], ACT.Exp).then_inc(dec_exp, 1)
            act.wait_ge(trb_ready, g + 1)
            if before:
                act.wait_ge(st_ready, g)
            nc.scalar.activation(btok[:].rearrange("p c n -> p (c n)"), b_norm[:], ACT.Copy).then_inc(btok_ready, 1)
            act.wait_ge(seg_ready, g + 1)
            nc.scalar.activation(m_t[:], m_t[:], ACT.Exp).then_inc(seg_exp, 1)
            ahead(split_hi, act, MIX, 8 + 6 * g, 8)
            act.wait_ge(evac["in"], 6 * g + 7)
            silu(zs[:, 1, :], zs[:, 1, :])

        def add_y_squares(pool, g):
            pool.wait_ge(ysq_ready, 2 * g)
            nc.gpsimd.tensor_tensor(yt[:, 0, :], yt[:, 0, :], yt[:, 1, :], ALU.add).then_inc(ysq_added, 1)

        def mix_pool(pool, g, first=False):
            for c in range(6):
                ahead(split_lo, pool, MIX, 3 + c + 6 * g, 3 + c)
                if c == 0 and not first:
                    add_y_squares(pool, g)
                if c == 4:
                    pool.wait_ge(silu_ready, 6 * g + 4)
                    pool.wait_ge(ecs_in, 16 * g + 16)
                    if not first:
                        pool.wait_ge(y_ready, g)
                    nc.gpsimd.tensor_tensor(cs_t[:], cT[:, P:S].unsqueeze(1).to_broadcast([P, HG, S - P]),
                                            ecs_bc[:, :, P:S], ALU.mult).then_inc(cs_ready, 1)

        def y_at(k):
            return ybuf[:, k, :]

        def mix_conv(dve, g, c, first):
            if not (first and c == 0):
                dve.wait_ge(silu_ready, 6 * g + c if c else 6 * g - 2)
            conv(dve, MIX, 1 + 6 * g + c, 1 + c, ug_s, SSM_T, SSM0 + SSMW * g + (SSM_T + 1) * c, cv_s[:], 4 * g + c)

        def y_gate_dve(dve, g):
            dve.wait_ge(y_ready, g)
            dve.wait_ge(skip_ready, 2 * g)
            dve.wait_ge(silu_ready, 6 * g)
            for jj in range(2):
                ch(nc.vector.tensor_tensor(yt[:, jj, :], b_y[:, jj, :], yt[:, jj, :], ALU.add))
            for jj in range(2):
                dve.wait_ge(dve_done, ch.value() - 1 + jj)
                nc.vector.tensor_tensor(y_at(2 * g - 2 + jj), yt[:, jj, :], zs[:, jj, :], ALU.mult).then_inc(y_gated, 1)

        def y_norm_dve(dve, g):
            dve.wait_ge(bc_ready, norm_no["group"] + g)
            dve.wait_ge(y_gated, 2 * g)
            dve.wait_ge(ysq_ready, 2 * g)
            for jj in range(2):
                nc.vector.scalar_tensor_tensor(
                    y_at(2 * g - 2 + jj), y_at(2 * g - 2 + jj),
                    col(SSM0 + SSMW * (g - 1) + 4 * (SSM_T + 1) + 2 + jj), b_norm[:],
                    ALU.mult, ALU.mult).then_inc(y_normed, 1)

        def dt_dve(dve):
            def step(ins):
                ch(ins)
                dve.wait_ge(dve_done, ch.value())

            dve.wait_ge(dtv_back, 1)
            step(nc.vector.tensor_copy(t_v[:], b_cb[:, 0:NB * HS]))
            nc.vector.scalar_tensor_tensor(t_w[:], t_v[:], -1.0, t_v[:], ALU.mult, ALU.min).then_inc(dt_in, 1)
            dve.wait_ge(dt_exp, 1)
            step(nc.vector.tensor_scalar(t_p[:], t_e[:], 2.0, None, ALU.add))
            step(nc.vector.reciprocal(t_p[:], t_p[:]))
            step(nc.vector.tensor_tensor(t_z[:], t_e[:], t_p[:], ALU.mult))
            step(nc.vector.tensor_tensor(t_w[:], t_z[:], t_z[:], ALU.mult))
            step(nc.vector.tensor_scalar(t_p[:], t_w[:], 1.0 / 15, None, ALU.mult))
            for k in (13, 11, 9, 7, 5, 3):
                step(nc.vector.scalar_tensor_tensor(t_p[:], t_p[:], 1.0 / k, t_w[:], ALU.add, ALU.mult))
            step(nc.vector.scalar_tensor_tensor(t_p[:], t_p[:], 1.0, t_z[:], ALU.add, ALU.mult))
            step(nc.vector.tensor_scalar(t_v[:], t_v[:], 0.0, None, ALU.max))
            nc.vector.scalar_tensor_tensor(dt_tok[:].rearrange("p c h -> p (c h)"), t_p[:], 2.0, t_v[:],
                                           ALU.mult, ALU.add).then_inc(dt_ready, 1)

        def acs_dve(dve):
            dve.wait_ge(al_exp, 1)
            dve.wait_ge(dt_back, 1)
            ch(nc.vector.tensor_scalar(d_e[:], b_cb[0:HS, :], d_ea[:], -1.0, ALU.mult, ALU.mult))
            dve.wait_ge(dve_done, ch.value())
            for c in range(NB):
                ins = nc.vector.tensor_tensor_scan(d_acs[:, c * P:(c + 1) * P], ones[0:HS, :],
                                                   d_e[:, c * P:(c + 1) * P], 0.0, ALU.mult, ALU.add)
            ins.then_inc(acs_ready, 1)

        def mix_dve(dve, g, first=False, proj=True, before=True, mid=None):
            if proj:
                mix_conv(dve, g, 0, first)
                if first:
                    dt_dve(dve)
            if before:
                y_gate_dve(dve, g)
            if proj:
                mix_conv(dve, g, 1, first)
                if first:
                    acs_dve(dve)
                mix_conv(dve, g, 2, first)
            if mid is not None:
                mid()
            if before:
                norm_diag(dve, norm_no["group"] + g - 1, split=True)
            if proj:
                mix_conv(dve, g, 3, first)
                if first:
                    dve.wait_ge(dtr_ready, 1)
                    ch(nc.vector.tensor_scalar(nacs[:].rearrange("p c h -> p (c h)"), b_cb[:, 0:NB * HS],
                                               -1.0, None, ALU.mult))
                    nc.vector.tensor_copy(acs_tok[:].rearrange("p c h -> p (c h)"),
                                          b_cb[:, 0:NB * HS]).then_inc(tok_ready, 1)
            if proj:
                dve.wait_ge(unit_done, 6 * g + 6)
                nc.vector.tensor_tensor(zs[:, 0, :], acc_of(MIX, 5)[:], r_pre[:], ALU.mult).then_inc(evac["in"], 1)
                if first:
                    dve.wait_ge(tot_ready, 1)
                    dve.wait_ge(dve_done, ch.value())
                    nc.vector.tensor_tensor(wdec[:].rearrange("p c h -> p (c h)"), b_cb[:, 0:NB * HS],
                                            nacs[:].rearrange("p c h -> p (c h)"), ALU.add).then_inc(dec_in, 1)
            if before:
                y_norm_dve(dve, g)
            if not proj:
                return
            if not first:
                dve.wait_ge(seg_ready, g)
            ch(nc.vector.tensor_copy(nac_g[:], nacs[:, :, bass.ds(HG * g, HG)]))
            dve.wait_ge(dve_done, ch.value())
            dve.wait_ge(acs_in, 16 * g + 16)
            if not first:
                dve.wait_ge(y_ready, g)
            for hh in range(HG):
                for c in range(NB):
                    ins = nc.vector.tensor_scalar(m_t[:, hh, c * P:(c + 1) * P], acs_bc[:, hh, c * P:(c + 1) * P],
                                                  nac_g[:, c, hh:hh + 1], 0.0, ALU.add, ALU.min)
            ins.then_inc(seg_ready, 1)
            if first:
                dve.wait_ge(dec_exp, 1)
                ch(nc.vector.tensor_tensor(wdec[:], wdec[:], dt_tok[:], ALU.mult))
                dve.wait_ge(dve_done, ch.value())
            dve.wait_ge(trx_ready, g + 1)
            if not first:
                dve.wait_ge(st_ready, g)
            for wgt, dst in ((dt_tok, xdt), (wdec, xdd)):
                for half in range(2):
                    ins = nc.vector.tensor_tensor(
                        dst[:, 2 * half:2 * half + 2, :, :],
                        b_x[:, half, :].rearrange("p (c h d) -> p c h d", c=2, h=HG),
                        wgt[:, 2 * half:2 * half + 2, bass.ds(HG * g, HG)].unsqueeze(3).to_broadcast([P, 2, HG, HD]),
                        ALU.mult)
            ins.then_inc(xw_ready, 1)
            dve.wait_ge(cb_ready, g + 1)
            if not first:
                dve.wait_ge(m_ready, g)
            nc.vector.tensor_tensor(cbm[:].rearrange("p (c l) -> p c l", c=NB),
                                    b_cb[:].rearrange("p (c l) -> p c l", c=NB),
                                    tri[:].unsqueeze(1).to_broadcast([P, NB, P]), ALU.mult).then_inc(cbm_ready, 1)
            dve.wait_ge(unit_done, 6 * g + 7)
            nc.vector.tensor_tensor(zs[:, 1, :], acc_of(MIX, 6)[:], r_pre[:], ALU.mult).then_inc(evac["in"], 1)
            dve.wait_ge(st_ready, g + 1)
            dve.wait_ge(ecs_in, 16 * g + 16)
            if not first:
                dve.wait_ge(prev_ready, g)

            def st(c):
                return b_x[:, c // 2, (c % 2) * 2 * P:(c % 2) * 2 * P + 2 * P].rearrange("p (h d) -> p h d", h=HG)

            ch(nc.vector.tensor_copy(prev[:, 0, :, :], st(0)))
            for c in range(1, NB - 1):
                dve.wait_ge(dve_done, ch.value())
                ch(nc.vector.tensor_tensor(
                    pdec[:], prev[:, c - 1, :, :],
                    ecs_bc[:, :, (c + 1) * P - 1:(c + 1) * P].to_broadcast([P, HG, HD]), ALU.mult))
                dve.wait_ge(dve_done, ch.value())
                ins = nc.vector.tensor_tensor(prev[:, c, :, :], pdec[:], st(c), ALU.add)
                if c < NB - 2:
                    ch(ins)
            ins.then_inc(prev_ready, 1)
            dve.wait_ge(seg_exp, g + 1)
            dve.wait_ge(cbm_ready, g + 1)
            nc.vector.tensor_tensor(m_t[:], m_t[:], cbm[:].unsqueeze(1).to_broadcast([P, HG, S]),
                                    ALU.mult).then_inc(m_ready, 1)

        def y_split_act(act, ks):
            for k in ks:
                nc.scalar.activation(y_hi[:, k, :], y_at(k), ACT.Copy).then_inc(yhi_ready, 1)

        def y_split_dve(dve, ks):
            for k in ks:
                dve.wait_ge(yhi_ready, k + 1)
                nc.vector.tensor_tensor(y_lo[:, k, :], y_at(k), y_hi[:, k, :].bitcast(F32),
                                        ALU.subtract).then_inc(ylo_ready, 1)

        def ffn_pe(pe, up, dn, layer):
            with pe.Fori(1, FC) as m:
                in_unit(pe, up, 2 * m, 0)
                in_unit(pe, up, 2 * m + 1, 1)
            out_halves_pe(pe, dn, 0, h_hi, h_lo, HU, ready=lambda k: pe.wait_ge(hlo_ready, layer * FC + k + 1))
            with pe.Fori(1, KC // 2) as i:
                out_halves_pe(pe, dn, i, h_hi, h_lo, HU)

        def ffn_act(act, up, layer):
            def hidden_hi(m):
                act.wait_ge(hb_ready, layer * FC + m + 1)
                nc.scalar.activation(h_hi[:, m, :], hb[:], ACT.Copy).then_inc(hhi_ready, 1)

            def pair(m, first=False):
                if not first:
                    ahead(split_hi, act, up, 2 * m + 2, 2)
                    hidden_hi(m - 1)
                act.wait_ge(conv_ready, 4 * NG + layer * 2 * FC + 2 * m + 1)
                if not (first and layer == 0):
                    act.wait_ge(hb_ready, layer * FC + m)
                nc.scalar.activation(sg[:], cg[:], ACT.Silu).then_inc(gate_ready, 1)
                ahead(split_hi, act, up, 2 * m + 3, 3)

            pair(0, True)
            with act.Fori(1, FC - 1) as m:
                pair(m)
            pair(FC - 1)
            hidden_hi(FC - 1)

        def ffn_pool(pool, up):
            ahead(split_lo, pool, up, 3)
            with pool.Fori(1, FC - 1) as m:
                ahead(split_lo, pool, up, 2 * m + 2, 2)
                ahead(split_lo, pool, up, 2 * m + 3, 3)
            ahead(split_lo, pool, up, up.units)
            ahead(split_lo, pool, up, up.units + 1)

        def ffn_dve(dve, up, layer):
            base = layer * FC

            def hidden_lo(m):
                dve.wait_ge(hhi_ready, base + m + 1)
                nc.vector.tensor_tensor(h_lo[:, m, :], hb[:], h_hi[:, m, :].bitcast(F32),
                                        ALU.subtract).then_inc(hlo_ready, 1)

            def pair(m, first=False):
                n_conv = 4 * NG + 2 * base + 2 * m
                w = FFN0 + FFNW * base + FFNW * m
                if not (first and layer == 0):
                    dve.wait_ge(gate_ready, base + m)
                conv(dve, up, 2 * m, 0, ug_f, FFN_T, w, cg[:], n_conv)
                if not first:
                    hidden_lo(m - 1)
                if not (first and layer == 0):
                    dve.wait_ge(hb_ready, base + m)
                conv(dve, up, 2 * m + 1, 1, ug_f, FFN_T, w + FFN_T + 1, cu[:], n_conv + 1)
                dve.wait_ge(conv_ready, n_conv + 2)
                dve.wait_ge(gate_ready, base + m + 1)
                if not (first and layer == 0):
                    dve.wait_ge(hlo_ready, base + m)
                nc.vector.tensor_tensor(hb[:], sg[:], cu[:], ALU.mult).then_inc(hb_ready, 1)

            memzero = nc.vector.memset(ug_f[:, 0:FFN_T - 1], 0.0)
            ch(memzero)
            dve.wait_ge(dve_done, ch.value())
            pair(0, True)
            with dve.Fori(1, FC) as m, ch.loop(m, 1, FC - 1, 2 * (FFN_T - 1)):
                pair(m)
            hidden_lo(FC - 1)

        def use(h, name):
            if isinstance(h, int) and h == 1:
                return {"v": 0, "t0": 1, "t1": 2}[name]
            return 5 * h + (3 - 10) + {"t2": 0, "t3": 1, "v": 2, "t0": 3, "t1": 4}[name]

        def aout_start(pe, c):
            if c == 0:
                for j in range(2):
                    pe.wait_ge(lo_made, AOUT.U0 + j + 1)
                    wait_bank(pe, AOUT, j)
            pe.wait_ge(olo_ready, c + 1)
            for j in range(2):
                last = product(acc_of(AOUT, j), slot_of(AOUT, j), c, o_hi[:, c, :], o_lo[:, c, :],
                               c == 0, c == KC - 1)
                if c == KC - 1:
                    last.then_inc(unit_done, 1)

        def att_pe(pe, h, b):
            proj = not (isinstance(h, int) and h >= NH)
            one = not (isinstance(h, int) and not 1 <= h <= NH)
            two = not (isinstance(h, int) and h < 2)
            rep = 3 * b
            b1, b2 = 1 - b, b

            def bank_free(name):
                n = use(h, name)
                if not (isinstance(n, int) and n == 0):
                    pe.wait_ge(tr_copied, n)

            def scores(i):
                n, keys = 4 * (h - 1) + i, (i + 1) * P
                if not (isinstance(n, int) and n < 2):
                    pe.wait_ge(s_taken, n - 1)
                for t in range(2):
                    last = nc.tensor.matmul(scores_in[i % 2][:, t, 0:keys],
                                            qT[DH * t:DH * t + DH, b1, i * P:(i + 1) * P],
                                            kT[DH * t:DH * t + DH, b1, 0:keys], start=True, stop=True)
                last.then_inc(s_ready, 1)

            def weights_back(i, name, a):
                bank_free(name)
                pe.wait_ge(a_ready, 4 * a + i + 1)
                for jb in range(i + 1):
                    last = nc.tensor.transpose(b_tr[:, jb * P:(jb + 1) * P], at[:, i, jb * P:(jb + 1) * P],
                                               ident[:])
                last.then_inc(tr_ready, 1)

            def filler(*cs):
                if not proj:
                    for c in cs:
                        aout_start(pe, c)

            late = isinstance(h, int) and h == NH + 1
            if proj and not (isinstance(h, int) and h == 0):
                in_unit(pe, QKV, 3 * h, rep)
            if two:
                weights_back(2, "t2", h - 2)
            if one:
                pe.wait_ge(evac["in"], QKV.before["in"] + 3 * h)
                scores(0)
                scores(1)
            filler(4 if late else 0)
            if two:
                weights_back(3, "t3", h - 2)
            if proj and not (isinstance(h, int) and h == 0):
                in_unit(pe, QKV, 3 * h + 1, rep + 1)
            filler(5 if late else 1)
            if one:
                bank_free("v")
                for c in range(NB):
                    last = nc.tensor.transpose(b_tr[:, c * P:(c + 1) * P], vT[:, b1, c * P:(c + 1) * P], ident[:])
                last.then_inc(tr_ready, 1)
            if two:
                pe.wait_ge(tr_copied, use(h, "t3") + 1)
                for jb in range(NB):
                    last = nc.tensor.matmul(b_pv[:, jb * P:S], vtok[:, b2, jb, :], aT[:, jb, jb * P:S],
                                            start=jb == 0, stop=jb == NB - 1)
                last.then_inc(pv_ready, 1)
            if one:
                scores(2)
                scores(3)
            filler(6 if late else 2)
            if two:
                pe.wait_ge(ob_ready, h - 1)
                norm_stat(osq, 2)
            if proj:
                in_unit(pe, QKV, 3 * h + 2, rep + 2)
            if one:
                weights_back(0, "t0", h - 1)
            if not late:
                filler(3)
            if two:
                norm_bcast(pe, norm_no["head"] + h - 2, split=True)
            if one:
                weights_back(1, "t1", h - 1)

        def att_act(act, h, b):
            proj = not (isinstance(h, int) and h >= NH)
            one = not (isinstance(h, int) and not 1 <= h <= NH)
            two = not (isinstance(h, int) and h < 2)
            rep = 3 * b
            b1 = 1 - b

            def probs(i):
                n, keys, sl = 4 * (h - 1) + i, (i + 1) * P, i % 2
                act.wait_ge(mx_ready, n + 1)
                if not (isinstance(n, int) and n < 2):
                    act.wait_ge(a_ready, n - 1)
                for t in range(2):
                    ins = nc.scalar.activation(pr[:, sl, t, 0:keys], sc[:, sl, t, 0:keys], ACT.Exp,
                                               bias=nmx[:, sl, t:t + 1], accum_out=den[:, sl, t:t + 1])
                ins.then_inc(p_ready, 1)

            def copy_back(i, name, a):
                act.wait_ge(tr_ready, use(h, name) + 1)
                if name == "t0" and not (isinstance(a, int) and a == 0):
                    act.wait_ge(pv_ready, a)
                nc.scalar.activation(aT[:, 0:i + 1, i * P:(i + 1) * P],
                                     b_tr[:, 0:(i + 1) * P].rearrange("p (j q) -> p j q", j=i + 1),
                                     ACT.Copy).then_inc(tr_copied, 1)

            if two:
                copy_back(2, "t2", h - 2)
            if proj and not (isinstance(h, int) and h == 0):
                ahead(split_hi, act, QKV, 3 * h + 2, rep + 2)
            if two:
                copy_back(3, "t3", h - 2)
            if one:
                probs(0)
                probs(1)
            if proj:
                ahead(split_hi, act, QKV, 3 * h + 3, rep + 3)
            if isinstance(h, int) and h == 0:
                act.wait_ge(lam_dots, 1)
                nc.scalar.activation(lam_s[:, 2:4], lam_s[:, 0:2], ACT.Exp).then_inc(lam_exps, 1)
            if one:
                act.wait_ge(tr_ready, use(h, "v") + 1)
                nc.scalar.activation(vtok[:, b1, :, :].rearrange("p c e -> p (c e)"), b_tr[:],
                                     ACT.Copy).then_inc(tr_copied, 1)
            if two:
                act.wait_ge(pv_ready, h - 1)
                nc.scalar.activation(ob[:], b_pv[:], ACT.Copy)
                nc.scalar.activation(osq[:], b_pv[:], ACT.Square).then_inc(ob_ready, 1)
                norm_root(act, norm_no["head"] + h - 2)
            if one:
                probs(2)
                probs(3)
                copy_back(0, "t0", h - 1)
            if proj:
                ahead(split_hi, act, QKV, 3 * h + 4, rep + 4)
            if one:
                copy_back(1, "t1", h - 1)
            if two:
                act.wait_ge(on_ready, h - 1)
                nc.scalar.activation(o_hi[:, h - 2, :], on[:], ACT.Copy).then_inc(ohi_ready, 1)

        def att_dve(dve, h, b):
            proj = not (isinstance(h, int) and h >= NH)
            one = not (isinstance(h, int) and not 1 <= h <= NH)
            two = not (isinstance(h, int) and h < 2)
            rep = 3 * b

            def take(j, dst):
                dve.wait_ge(unit_done, QKV.U0 + 3 * h + j + 1)
                if dst is qT:
                    ins = nc.vector.scalar_tensor_tensor(dst[:, b, :], acc_of(QKV, rep + j)[:], DH ** -0.5,
                                                         r_pre[:], ALU.mult, ALU.mult)
                else:
                    ins = nc.vector.tensor_tensor(dst[:, b, :], acc_of(QKV, rep + j)[:], r_pre[:], ALU.mult)
                ins.then_inc(evac["in"], 1)

            def biased(i):
                n, keys, sl = 4 * (h - 1) + i, (i + 1) * P, i % 2
                dve.wait_ge(s_ready, n + 1)
                if not (isinstance(n, int) and n < 2):
                    dve.wait_ge(p_ready, n - 1)
                nc.vector.scalar_tensor_tensor(
                    sc[:, sl, :, 0:keys], dist[:, S - keys:S].unsqueeze(1).to_broadcast([P, 2, keys]),
                    slopes[:, bass.ds(h - 1, 1)], scores_in[sl][:, :, 0:keys], ALU.mult, ALU.add).then_inc(s_taken, 1)
                dve.wait_ge(s_taken, n + 1)
                nc.vector.tensor_reduce(nmx[:, sl, :], sc[:, sl, :, 0:keys], AX.X, ALU.max,
                                        negate=True).then_inc(mx_ready, 1)

            def combine(i):
                n, keys, sl = 4 * (h - 1) + i, (i + 1) * P, i % 2
                dve.wait_ge(p_ready, n + 1)
                if not (isinstance(n, int) and n < 2):
                    dve.wait_ge(a_ready, n - 1)
                if not (isinstance(h, int) and h == 1):
                    dve.wait_ge(tr_ready, (use(h - 1, f"t{i}") if i < 2 else use(h, f"t{i}")) + 1)
                ch(nc.vector.reciprocal(cf[:, sl, :], den[:, sl, :]))
                dve.wait_ge(dve_done, ch.value())
                ch(nc.vector.tensor_scalar(cf[:, sl, 1:2], cf[:, sl, 1:2], lam_s[:, 4:5], None, ALU.mult))
                ch(nc.vector.tensor_scalar(at[:, i, 0:keys], pr[:, sl, 0, 0:keys], cf[:, sl, 0:1], None, ALU.mult))
                dve.wait_ge(dve_done, ch.value())
                nc.vector.scalar_tensor_tensor(at[:, i, 0:keys], pr[:, sl, 1, 0:keys], cf[:, sl, 1:2],
                                               at[:, i, 0:keys], ALU.mult, ALU.add).then_inc(a_ready, 1)

            if proj:
                take(0, qT)
            if isinstance(h, int) and h == 1:
                dve.wait_ge(dist_made, 3)
                dve.wait_ge(lam_exps, 1)
                ch(nc.vector.tensor_tensor(lam_s[:, 4:5], lam_s[:, 3:4], lam_s[:, 2:3], ALU.subtract))
                dve.wait_ge(dve_done, ch.value())
                ch(nc.vector.tensor_scalar(lam_s[:, 4:5], lam_s[:, 4:5], -LAMBDA_INIT, None, ALU.add))
                dve.wait_ge(dve_done, ch.value())
            if one:
                biased(0)
                biased(1)
                combine(0)
                combine(1)
            if proj:
                take(1, kT)
            if one:
                biased(2)
                biased(3)
            if two:
                norm_diag(dve, norm_no["head"] + h - 2, split=True)
            if one:
                combine(2)
            if proj:
                take(2, vT)
            if two:
                dve.wait_ge(bc_ready, norm_no["head"] + h - 1)
                nc.vector.scalar_tensor_tensor(on[:], ob[:], gsub[:], b_norm[:], ALU.mult,
                                               ALU.mult).then_inc(on_ready, 1)
            if one:
                combine(3)
            if two:
                dve.wait_ge(ohi_ready, h - 1)
                nc.vector.tensor_tensor(o_lo[:, h - 2, :], on[:], o_hi[:, h - 2, :].bitcast(F32),
                                        ALU.subtract).then_inc(olo_ready, 1)
                dve.wait_ge(olo_ready, h - 1)

        def att_rounds(eng, part, chained=None):
            part(eng, 0, 0)
            part(eng, 1, 1)
            with eng.Fori(1, NH // 2) as i:
                if chained is None:
                    part(eng, 2 * i, 0)
                    part(eng, 2 * i + 1, 1)
                else:
                    with ch.loop(i, 1, NH // 2 - 1, chained):
                        part(eng, 2 * i, 0)
                        part(eng, 2 * i + 1, 1)
            part(eng, NH, 0)
            part(eng, NH + 1, 1)

        block = ctx.enter_context(nc.Block())

        @block.sync
        def _(sp):
            load_unit(sp, MIX, 0, 0)
            sp.dma_start(par[:], params).then_inc(par_in, 16)
            load_unit(sp, MIX, 1, 1)
            for m in range(KC):
                sp.dma_start(x[:, m, :], x_in[:, m, :]).then_inc(x_in_s[m], 16)
            sp.dma_start(lam_v[:], lam_in.partition_broadcast(P)).then_inc(lam_in_s, 16)

            def group(g, first=False):
                for c in range(6):
                    if c == 4:
                        if first:
                            load_unit(sp, MIX, 1 + c, 1 + c)
                            sp.wait_ge(acs_ready, 1)
                            sp.dma_start(scratch[0], d_acs[:]).then_inc(acs_out, 16)
                            sp.wait_ge(ecs_ready, 1)
                            sp.dma_start(scratch[1], d_z[:]).then_inc(ecs_out, 16)
                            sp.wait_ge(acs_out, 16)
                            sp.wait_ge(ecs_out, 16)
                        else:
                            sp.wait_ge(seg_ready, g)
                            sp.wait_ge(prev_ready, g)
                            sp.wait_ge(cs_ready, g)
                        for k, (dst, done) in enumerate(((acs_bc, acs_in), (ecs_bc, ecs_in))):
                            rows = scratch[k, bass.ds(HG * g, HG), :]
                            sp.dma_start(dst[:], rows.partition_broadcast(P)).then_inc(done, 16)
                    if not (first and c in (0, 4)):
                        load_unit(sp, MIX, 1 + 6 * g + c, 1 + c)

            group(0, True)
            with sp.Fori(1, NG) as g:
                group(g)
            for ph in PH[1:]:
                with sp.Fori(0, ph.units // 2) as i:
                    load_unit(sp, ph, 2 * i, 0)
                    load_unit(sp, ph, 2 * i + 1, 1)
            for m in range(KC):
                wait_x(sp, 4, m)
                sp.dma_start(out[:, m, :], x[:, m, :]).then_inc(y_sent, 16)
            sp.wait_ge(y_sent, 16 * KC)

        @block.gpsimd
        def _(pool):
            n = 0

            def const(ins):
                nonlocal n
                ins.then_inc(consts, 1)
                n += 1

            def picked(tile, base, step, cmp, fill, width=P):
                pool.wait_ge(consts, n)
                const(nc.gpsimd.affine_select(out=tile, in_=tile, compare_op=cmp, fill=fill, base=base,
                                              pattern=[[step, width]], channel_multiplier=1))

            const(nc.gpsimd.memset(ident[:], 0.0))
            picked(ident[:], 0, -1, ALU.not_equal, 1.0)
            const(nc.gpsimd.memset(ones[:], 1.0))
            const(nc.gpsimd.memset(eps[:], EPS))
            for i, width in enumerate((D, DI // NG, 2 * DH)):
                const(nc.gpsimd.memset(mean_col[:, i:i + 1], 1.0 / width))
            for h in range(NH):
                const(nc.gpsimd.memset(slopes[:, h:h + 1], 2.0 ** (-8.0 * (h + 1) / NH)))
            const(nc.gpsimd.memset(tri[:], 0.0))
            picked(tri[:], 0, -1, ALU.is_gt, 1.0)
            const(nc.gpsimd.memset(last_row[:], 0.0))
            picked(last_row[:], -(P - 1), 0, ALU.not_equal, 1.0)
            assert n == N_CONST, n

            boundary_pool(pool, 0, MIX)
            mix_pool(pool, 0, first=True)
            with pool.Fori(1, NG) as g:
                mix_pool(pool, g)
            add_y_squares(pool, NG)
            out_phase_pool(pool, SOUT, out_halves, 1, UP0)
            ffn_pool(pool, UP0)
            out_phase_pool(pool, DN0, out_halves, 2, QKV)
            def distances():
                nc.gpsimd.iota(dist_i[:], [[1, S]], base=P - S, channel_multiplier=-1).then_inc(dist_made, 1)
                pool.wait_ge(dist_made, 1)
                nc.gpsimd.tensor_copy(dist[:], dist_i[:]).then_inc(dist_made, 1)
                pool.wait_ge(dist_made, 2)
                nc.gpsimd.affine_select(out=dist[:], in_=dist[:], compare_op=ALU.is_ge, fill=MASKED, base=S - P,
                                        pattern=[[-1, S]], channel_multiplier=1).then_inc(dist_made, 1)

            def att_pool(eng, h, b):
                for j in range(3):
                    if not (isinstance(h, int) and (h >= NH or h + j == 0)):
                        ahead(split_lo, eng, QKV, 3 * h + 2 + j, 3 * b + 2 + j)
                        if isinstance(h, int) and h == 0 and j == 1:
                            distances()
            att_rounds(pool, att_pool)
            out_phase_pool(pool, AOUT, out_wholes, 3, UP1)
            ffn_pool(pool, UP1)
            out_phase_pool(pool, DN1, out_halves, 4)

        @block.scalar
        def _(act):
            act.wait_ge(consts, N_CONST)
            split_hi(act, MIX, 0, 0)
            split_hi(act, MIX, 1, 1)
            act.wait_ge(par_in, 16)
            boundary_act(act, 0, MIX)
            mix_act(act, 0, first=True, before=False)
            with act.Fori(1, NG) as g:
                mix_act(act, g)
            act.wait_ge(y_normed, 2 * NG - 2)
            act.wait_ge(seg_ready, NG)
            act.wait_ge(prev_ready, NG)
            act.wait_ge(cs_ready, NG)
            y_split_act(act, range(YC // 2))
            def mid(done):
                if not done:
                    y_split_act(act, range(YC // 2, YC - 2))
                ahead(split_hi, act, SOUT, 2 + done)

            mix_act(act, NG, proj=False, mid=mid)
            for k in range(YC - 2, YC):
                act.wait_ge(y_normed, k + 1)
                y_split_act(act, [k])
            out_phase_act(act, SOUT, out_halves, 1, UP0)
            ffn_act(act, UP0, 0)
            out_phase_act(act, DN0, out_halves, 2, QKV)
            att_rounds(act, att_act)
            out_phase_act(act, AOUT, out_wholes, 3, UP1)
            ffn_act(act, UP1, 1)
            out_phase_act(act, DN1, out_halves, 4)

        @block.vector
        def _(dve):
            dve.wait_ge(par_in, 16)
            dve.wait_ge(consts, N_CONST)
            ch(nc.vector.memset(ug_s[:, 0:SSM_T - 1], 0.0))
            ch(nc.vector.tensor_copy(ones_r[:], ones[:]))
            split_lo_dve(dve, MIX, 0)
            split_lo_dve(dve, MIX, 1)
            boundary_dve(dve, 0, MIX)
            dve.wait_ge(unit_done, 1)
            nc.vector.tensor_tensor(d_v[:], bank[0][0:HS, :], r_pre[0:HS, :], ALU.mult).then_inc(evac["in"], 1)
            dve.wait_ge(evac["in"], 1)
            nc.vector.tensor_scalar(d_v[:], d_v[:], par[0:HS, DTB:DTB + 1], None, ALU.add).then_inc(dtv_ready, 1)
            mix_dve(dve, 0, first=True, before=False)
            with dve.Fori(1, NG) as g, ch.loop(g, 1, NG - 1, MIX_CHAIN):
                mix_dve(dve, g)
            y_split_dve(dve, range(YC // 2))
            mix_dve(dve, NG, proj=False, mid=lambda: y_split_dve(dve, range(YC // 2, YC - 2)))
            y_split_dve(dve, range(YC - 2, YC))
            boundary_dve(dve, 1, UP0)
            ffn_dve(dve, UP0, 0)
            dve.wait_ge(lam_in_s, 16)
            ch(nc.vector.tensor_tensor(lam_p[:], lam_v[:, 0:2 * DH], lam_v[:, 2 * DH:4 * DH], ALU.mult))
            dve.wait_ge(dve_done, ch.value())
            nc.vector.tensor_reduce(lam_s[:, 0:2], lam_p[:].rearrange("p (a d) -> p a d", a=2), AX.X,
                                    ALU.add).then_inc(lam_dots, 1)
            ch(nc.vector.tensor_scalar(gsub[:], par[:, SUBLN:SUBLN + 1], 1.0 - LAMBDA_INIT, None, ALU.mult))
            boundary_dve(dve, 2, QKV)
            att_rounds(dve, att_dve, chained=ATT_CHAIN)
            boundary_dve(dve, 3, UP1)
            ffn_dve(dve, UP1, 1)
            boundary_dve(dve, 4)

        @block.tensor
        def _(pe):
            pe.wait_ge(consts, N_CONST)
            boundary_pe(pe, 0, MIX)
            mix_pe(pe, 0, skip_x0=True, before=False)
            with pe.Fori(1, NG) as g:
                mix_pe(pe, g)

            def mid(q):
                if q == 0:
                    pe.wait_ge(ysq_added, NG)
                    norm_stat(yt[:, 0, :], 1)
                elif q == 1:
                    norm_bcast(pe, norm_no["group"] + NG - 1, split=True)

            mix_y_pe(pe, NG)
            out_halves_pe(pe, SOUT, 0, y_hi, y_lo, KC, ready=lambda k: pe.wait_ge(ylo_ready, k + 1), mid=mid)
            with pe.Fori(1, KC // 2) as i:
                out_halves_pe(pe, SOUT, i, y_hi, y_lo, KC)
            boundary_pe(pe, 1, UP0)
            ffn_pe(pe, UP0, DN0, 0)
            boundary_pe(pe, 2, QKV)
            att_rounds(pe, att_pe)
            aout_start(pe, KC - 1)
            with pe.Fori(1, KC // 2) as i:
                for s in range(2):
                    pe.wait_ge(lo_made, AOUT.U0 + 2 * i + s + 1)
                    wait_bank(pe, AOUT, 2 * i + s)
                    for c in range(KC):
                        last = product(acc_of(AOUT, s), slot_of(AOUT, s), c, o_hi[:, c, :], o_lo[:, c, :],
                                       c == 0, c == KC - 1)
                    last.then_inc(unit_done, 1)
            boundary_pe(pe, 3, UP1)
            ffn_pe(pe, UP1, DN1, 1)
            boundary_pe(pe, 4)


def _tiles(w, cols, k0=0, k1=None):
    part = w[k0:k1, cols:cols + P]
    return part.reshape(-1, P, P).transpose(1, 0, 2).reshape(P, -1)


def _halves(w):
    k = w.shape[0] // 2
    return np.stack([_tiles(w, (2 * i + s) * P, h * k, (h + 1) * k)
                     for i in range(KC // 2) for h in range(2) for s in range(2)])


def _by_chunk(v):
    return v.reshape(-1, P).T


def _pack(a):
    par = np.zeros((P, NPAR), np.float32)
    for layer in range(2):
        for kind, name in enumerate(("norm_mix_pre", "norm_mix_post", "norm_ffn_pre", "norm_ffn_post")):
            c = NORM0 + (layer * 4 + kind) * KC
            par[:, c:c + KC] = _by_chunk(a[name][layer])
    cw, cb, d, ng = a["ssm_conv_w"][0], a["ssm_conv_b"][0], a["ssm_D"][0], a["ssm_norm_g"][0]
    for g in range(NG):
        c = SSM0 + g * SSMW
        for f in (2 * g * P, (2 * g + 1) * P, DI + g * P, DI + NG * P + g * P):
            par[:, c:c + SSM_T] = cw[:, f:f + P].T
            par[:, c + SSM_T] = cb[f:f + P]
            c += SSM_T + 1
        for jj in range(2):
            par[0:HD, c + jj] = d[HG * g + 2 * jj]
            par[HD:P, c + jj] = d[HG * g + 2 * jj + 1]
        par[:, c + 2:c + 4] = _by_chunk(ng[2 * g * P:2 * (g + 1) * P])
    for layer in range(2):
        cw, cb = a["ffn_conv_w"][layer], a["ffn_conv_b"][layer]
        for m in range(FC):
            for s, f in enumerate((m * P, DFF + m * P)):
                c = FFN0 + (layer * FC + m) * FFNW + s * (FFN_T + 1)
                par[:, c:c + FFN_T] = cw[:, f:f + P].T
                par[:, c + FFN_T] = cb[f:f + P]
    par[:, SUBLN] = a["attn_subln_g"][0]
    par[0:HS, DTB] = a["ssm_dt_bias"][0]
    par[0:HS, ALOG] = a["ssm_A_log"][0]
    return par


def kernel(**inputs):
    from concourse import bacc
    from concourse.bass_utils import run_bass_kernel_spmd

    a = {k: np.asarray(v) for k, v in inputs.items()}
    w = a["ssm_w_in"][0]
    dt_cols = np.zeros((D, P), np.float32)
    dt_cols[:, 0:HS] = w[:, 2 * DI + 2 * NG * P:]
    mix = [_tiles(dt_cols, 0)]
    for g in range(NG):
        for c in (DI + 2 * g * P, DI + (2 * g + 1) * P, 2 * DI + g * P, 2 * DI + NG * P + g * P,
                  2 * g * P, (2 * g + 1) * P):
            mix.append(_tiles(w, c))
    qkv, wo = a["attn_w_qkv"][0], a["attn_w_out"][0]
    arrays = {
        "x_in": a["x"][0].T.reshape(KC, P, S).transpose(1, 0, 2),
        "w_mix": np.stack(mix),
        "w_sout": _halves(a["ssm_w_out"][0]),
        "w_up0": np.stack([_tiles(a["ffn_w_up"][0], s * DFF + m * P) for m in range(FC) for s in range(2)]),
        "w_dn0": _halves(a["ffn_w_down"][0]),
        "w_qkv": np.stack([_tiles(qkv, c * D + h * P) for h in range(NH) for c in range(3)]),
        "w_aout": np.stack([_tiles(wo, m * P) for m in range(KC)]),
        "w_up1": np.stack([_tiles(a["ffn_w_up"][1], s * DFF + m * P) for m in range(FC) for s in range(2)]),
        "w_dn1": _halves(a["ffn_w_down"][1]),
        "params": _pack(a),
        "lam_in": np.concatenate([a["attn_lambda_q1"][0], a["attn_lambda_q2"][0],
                                  a["attn_lambda_k1"][0], a["attn_lambda_k2"][0]]),
    }
    arrays = {k: np.ascontiguousarray(v) for k, v in arrays.items()}
    nc = bacc.Bacc("TRN2", target_bir_lowering=False, num_devices=1)
    args = [nc.dram_tensor(k, v.shape, F32, kind="ExternalInput").ap() for k, v in arrays.items()]
    out = nc.dram_tensor("out", (P, KC, S), F32, kind="ExternalOutput").ap()
    trunk(nc, *args, out)
    got = run_bass_kernel_spmd(nc, [arrays], core_ids=[0]).results[0]["out"]
    return np.ascontiguousarray(got.transpose(1, 0, 2).reshape(D, S).T).reshape(1, S, D)
```
